# Optimizing a Trainium2 kernel written in Bass

```python
import math
import jax, jax.numpy as jnp
from jax import lax
import numpy as np

D_MODEL = 1024
BATCH = 1
SEQ = 1024
DEPTH = 2
DEC_BATCH = 1
DEC_SEQ = 64
PAST_LEN = 256

CHUNK = 64
Q_BLOCK = 128
N_EVEN = (DEPTH + 1) // 2
N_ODD = DEPTH // 2
HEAD_DIM = 64
H_A = 4
DK_A = HEAD_DIM
DV_A = 2 * HEAD_DIM
H_B = 8
DK_B = HEAD_DIM
H_C = D_MODEL // HEAD_DIM
C_PAST_CHUNKS = 8
C_BAND_PAST = C_PAST_CHUNKS * CHUNK
REL_CLIP = 256
D_FF = 4 * D_MODEL
NORM_EPS = 1e-6
A_QK = H_A * 2 * DK_A
A_V = H_A * DV_A
B_QK = H_B * DK_B
D_IN_EVEN = 2 * A_QK + A_V + 3 * B_QK + H_B
D_MIX = A_V + B_QK
NEG_INF = -1e30

kernel_name = 'hybrid_streaming_encoder_step'

def rmsnorm(x, g):
    xf = x.astype(jnp.float32)
    y = xf * lax.rsqrt(jnp.mean(xf * xf, axis=-1, keepdims=True) + NORM_EPS)
    return (y * g.astype(jnp.float32)).astype(x.dtype)

def alibi_slopes():
    return 2.0 ** (-8.0 * jnp.arange(1, H_A + 1, dtype=jnp.float32) / H_A)

def diff_attention(q, k, v, q_pos, k_pos, lam):
    s = jnp.einsum('bqhmd,bkhmd->bmhqk', q, k).astype(jnp.float32) * (DK_A ** -0.5)
    dist = jnp.abs(q_pos[:, None] - k_pos[None, :]).astype(jnp.float32)
    bias = -alibi_slopes()[:, None, None] * dist
    visible = (k_pos[None, :] // CHUNK) <= (q_pos[:, None] // CHUNK)
    p = jax.nn.softmax(jnp.where(visible, s + bias, NEG_INF), axis=-1)
    w = p[:, 0] - lam * p[:, 1]
    return jnp.einsum('bhqk,bkhd->bqhd', w.astype(v.dtype), v)

def forgetting_attention(q, k, v, cum_q, cum_k, q_pos, k_pos):
    s = jnp.einsum('bqhd,bkhd->bhqk', q, k).astype(jnp.float32) * (DK_B ** -0.5)
    decay = jnp.swapaxes(cum_q, 1, 2)[..., :, None] - jnp.swapaxes(cum_k, 1, 2)[..., None, :]
    visible = k_pos[None, :] <= q_pos[:, None]
    p = jax.nn.softmax(jnp.where(visible, s + decay, NEG_INF), axis=-1)
    return jnp.einsum('bhqk,bkhd->bqhd', p.astype(v.dtype), v)

def chunk_band_attention(q, k, v, q_pos, k_pos, table):
    s = jnp.einsum('bqhd,bkhd->bhqk', q, k).astype(jnp.float32) * (HEAD_DIM ** -0.5)
    rel = jnp.clip(q_pos[:, None] - k_pos[None, :], -REL_CLIP, REL_CLIP) + REL_CLIP
    bias = table.astype(jnp.float32)[:, rel]
    qc = q_pos[:, None] // CHUNK
    kc = k_pos[None, :] // CHUNK
    visible = (k_pos[None, :] >= 0) & (kc <= qc) & (kc >= qc - C_PAST_CHUNKS)
    p = jax.nn.softmax(jnp.where(visible, s + bias, NEG_INF), axis=-1)
    return jnp.einsum('bhqk,bkhd->bqhd', p.astype(v.dtype), v)

def diff_lambda(lq1, lk1, lq2, lk2, lam_init):
    f = jnp.float32
    return (jnp.exp(jnp.sum(lq1.astype(f) * lk1.astype(f)))
            - jnp.exp(jnp.sum(lq2.astype(f) * lk2.astype(f))) + lam_init)

def even_project(h, w_in, b_f):
    B, T, _ = h.shape
    z = h @ w_in
    cuts = np.cumsum([A_QK, A_QK, A_V, B_QK, B_QK, B_QK]).tolist()
    qa, ka, va, qb, kb, vb, fz = jnp.split(z, cuts, axis=-1)
    qa = qa.reshape(B, T, H_A, 2, DK_A)
    ka = ka.reshape(B, T, H_A, 2 * DK_A)
    va = va.reshape(B, T, H_A, DV_A)
    qb = qb.reshape(B, T, H_B, DK_B)
    kb = kb.reshape(B, T, H_B, DK_B)
    vb = vb.reshape(B, T, H_B, DK_B)
    logf = jax.nn.log_sigmoid(fz.astype(jnp.float32) + b_f.astype(jnp.float32))
    return qa, ka, va, qb, kb, vb, logf

def even_merge(oa, ob, subln_g, lam_init, w_out):
    B, T = oa.shape[:2]
    oa = rmsnorm(oa, subln_g) * (1.0 - lam_init)
    o = jnp.concatenate([oa.reshape(B, T, A_V), ob.reshape(B, T, B_QK)], axis=-1)
    return o @ w_out

def even_mixer_prompt(h, w_in, b_f, lam, subln_g, lam_init, w_out):
    B, T, _ = h.shape
    qa, ka, va, qb, kb, vb, logf = even_project(h, w_in, b_f)
    cum = jnp.cumsum(logf, axis=1)
    pos = jnp.arange(T, dtype=jnp.int32)
    ka5 = ka.reshape(B, T, H_A, 2, DK_A)

    def block(i):
        start = i * Q_BLOCK
        q_pos = start + jnp.arange(Q_BLOCK, dtype=jnp.int32)
        oa = diff_attention(lax.dynamic_slice_in_dim(qa, start, Q_BLOCK, axis=1), ka5, va, q_pos, pos, lam)
        ob = forgetting_attention(lax.dynamic_slice_in_dim(qb, start, Q_BLOCK, axis=1), kb, vb,
                                  lax.dynamic_slice_in_dim(cum, start, Q_BLOCK, axis=1), cum, q_pos, pos)
        return oa, ob

    oa, ob = lax.map(block, jnp.arange(T // Q_BLOCK, dtype=jnp.int32))
    oa = jnp.moveaxis(oa, 0, 1).reshape(B, T, H_A, DV_A)
    ob = jnp.moveaxis(ob, 0, 1).reshape(B, T, H_B, DK_B)
    return even_merge(oa, ob, subln_g, lam_init, w_out), (ka, va, kb, vb, logf)

def even_mixer_sample(h, c_ka, c_va, c_kb, c_vb, c_logf, w_in, b_f, lam, subln_g, lam_init, w_out):
    B, T, _ = h.shape
    P = c_ka.shape[1]
    qa, ka, va, qb, kb, vb, logf = even_project(h, w_in, b_f)
    ka_all = jnp.concatenate([c_ka, ka], axis=1).reshape(B, P + T, H_A, 2, DK_A)
    va_all = jnp.concatenate([c_va, va], axis=1)
    kb_all = jnp.concatenate([c_kb, kb], axis=1)
    vb_all = jnp.concatenate([c_vb, vb], axis=1)
    cum = jnp.cumsum(jnp.concatenate([c_logf.astype(jnp.float32), logf], axis=1), axis=1)
    q_pos = P + jnp.arange(T, dtype=jnp.int32)
    k_pos = jnp.arange(P + T, dtype=jnp.int32)
    oa = diff_attention(qa, ka_all, va_all, q_pos, k_pos, lam)
    ob = forgetting_attention(qb, kb_all, vb_all, cum[:, P:], cum, q_pos, k_pos)
    return even_merge(oa, ob, subln_g, lam_init, w_out), (ka, va, kb, vb, logf)

def odd_project(h, w_in):
    B, T, _ = h.shape
    q, k, v = jnp.split(h @ w_in, 3, axis=-1)
    return (q.reshape(B, T, H_C, HEAD_DIM), k.reshape(B, T, H_C, HEAD_DIM), v.reshape(B, T, H_C, HEAD_DIM))

def odd_mixer_prompt(h, w_in, table, w_out):
    B, T, _ = h.shape
    q, k, v = odd_project(h, w_in)
    pad = ((0, 0), (C_BAND_PAST, 0), (0, 0), (0, 0))
    kp = jnp.pad(k, pad)
    vp = jnp.pad(v, pad)
    band = C_BAND_PAST + CHUNK

    def chunk_fn(c):
        start = c * CHUNK
        q_pos = start + jnp.arange(CHUNK, dtype=jnp.int32)
        k_pos = start - C_BAND_PAST + jnp.arange(band, dtype=jnp.int32)
        return chunk_band_attention(lax.dynamic_slice_in_dim(q, start, CHUNK, axis=1),
                                    lax.dynamic_slice_in_dim(kp, start, band, axis=1),
                                    lax.dynamic_slice_in_dim(vp, start, band, axis=1),
                                    q_pos, k_pos, table)

    o = lax.map(chunk_fn, jnp.arange(T // CHUNK, dtype=jnp.int32))
    o = jnp.moveaxis(o, 0, 1).reshape(B, T, D_MODEL)
    W = min(C_BAND_PAST, T)
    return o @ w_out, (k[:, T - W:], v[:, T - W:])

def odd_mixer_sample(h, c_k, c_v, past_len, w_in, table, w_out):
    B, T, _ = h.shape
    W = c_k.shape[1]
    q, k, v = odd_project(h, w_in)
    k_all = jnp.concatenate([c_k, k], axis=1)
    v_all = jnp.concatenate([c_v, v], axis=1)
    q_pos = past_len + jnp.arange(T, dtype=jnp.int32)
    k_pos = past_len - W + jnp.arange(W + T, dtype=jnp.int32)
    o = chunk_band_attention(q, k_all, v_all, q_pos, k_pos, table).reshape(B, T, D_MODEL)
    return o @ w_out, (k_all[:, T:], v_all[:, T:])

def squared_relu_mlp(h, w_up, w_down):
    u = jax.nn.relu(h @ w_up)
    return (u * u) @ w_down

def setup_inputs(seed: int = 0) -> dict:
    key = jax.random.key(seed)
    ks = jax.random.split(key, 32)

    def nrm(k, shape, scale=1.0):
        return scale * jax.random.normal(k, shape, jnp.float32)

    w_c = min(C_BAND_PAST, PAST_LEN)
    return {
        'x_prompt': nrm(ks[0], (BATCH, SEQ, D_MODEL)),
        'x_sample': nrm(ks[1], (DEC_BATCH, DEC_SEQ, D_MODEL)),
        'cache_a_k': nrm(ks[2], (N_EVEN, DEC_BATCH, PAST_LEN, H_A, 2 * DK_A)),
        'cache_a_v': nrm(ks[3], (N_EVEN, DEC_BATCH, PAST_LEN, H_A, DV_A)),
        'cache_b_k': nrm(ks[4], (N_EVEN, DEC_BATCH, PAST_LEN, H_B, DK_B)),
        'cache_b_v': nrm(ks[5], (N_EVEN, DEC_BATCH, PAST_LEN, H_B, DK_B)),
        'cache_b_logf': jax.nn.log_sigmoid(2.0 + nrm(ks[6], (N_EVEN, DEC_BATCH, PAST_LEN, H_B), 0.5)),
        'cache_c_k': nrm(ks[7], (N_ODD, DEC_BATCH, w_c, H_C, HEAD_DIM)),
        'cache_c_v': nrm(ks[8], (N_ODD, DEC_BATCH, w_c, H_C, HEAD_DIM)),
        'w_in_even': nrm(ks[9], (N_EVEN, D_MODEL, D_IN_EVEN), D_MODEL ** -0.5),
        'b_forget': 2.0 + nrm(ks[10], (N_EVEN, H_B), 0.1),
        'lam_q1': nrm(ks[11], (N_EVEN, DK_A), 0.1),
        'lam_k1': nrm(ks[12], (N_EVEN, DK_A), 0.1),
        'lam_q2': nrm(ks[13], (N_EVEN, DK_A), 0.1),
        'lam_k2': nrm(ks[14], (N_EVEN, DK_A), 0.1),
        'subln_g': 1.0 + nrm(ks[15], (N_EVEN, DV_A), 0.05),
        'w_out_even': nrm(ks[16], (N_EVEN, D_MIX, D_MODEL), D_MIX ** -0.5),
        'w_in_odd': nrm(ks[17], (N_ODD, D_MODEL, 3 * D_MODEL), D_MODEL ** -0.5),
        'rel_bias': nrm(ks[18], (N_ODD, H_C, 2 * REL_CLIP + 1), 0.5),
        'w_out_odd': nrm(ks[19], (N_ODD, D_MODEL, D_MODEL), D_MODEL ** -0.5),
        'g_pre_mix': 1.0 + nrm(ks[20], (DEPTH, D_MODEL), 0.05),
        'g_post_mix': 1.0 + nrm(ks[21], (DEPTH, D_MODEL), 0.05),
        'g_pre_ffn': 1.0 + nrm(ks[22], (DEPTH, D_MODEL), 0.05),
        'g_post_ffn': 1.0 + nrm(ks[23], (DEPTH, D_MODEL), 0.05),
        'w_ffn_up': nrm(ks[24], (DEPTH, D_MODEL, D_FF), D_MODEL ** -0.5),
        'w_ffn_down': nrm(ks[25], (DEPTH, D_FF, D_MODEL), D_FF ** -0.5),
    }

def reference(x_prompt, x_sample, cache_a_k, cache_a_v, cache_b_k, cache_b_v, cache_b_logf,
              cache_c_k, cache_c_v, w_in_even, b_forget, lam_q1, lam_k1, lam_q2, lam_k2,
              subln_g, w_out_even, w_in_odd, rel_bias, w_out_odd, g_pre_mix, g_post_mix,
              g_pre_ffn, g_post_ffn, w_ffn_up, w_ffn_down):
    past_len = cache_b_logf.shape[2]
    xp, xs = x_prompt, x_sample
    even_p, even_s, odd_p, odd_s = [], [], [], []
    for l in range(DEPTH):
        hp = rmsnorm(xp, g_pre_mix[l])
        hs = rmsnorm(xs, g_pre_mix[l])
        if l % 2 == 0:
            e = l // 2
            lam_init = 0.8 - 0.6 * math.exp(-0.3 * l)
            lam = diff_lambda(lam_q1[e], lam_k1[e], lam_q2[e], lam_k2[e], lam_init)
            mp, rp = even_mixer_prompt(hp, w_in_even[e], b_forget[e], lam, subln_g[e], lam_init, w_out_even[e])
            ms, rs = even_mixer_sample(hs, cache_a_k[e], cache_a_v[e], cache_b_k[e], cache_b_v[e], cache_b_logf[e],
                                       w_in_even[e], b_forget[e], lam, subln_g[e], lam_init, w_out_even[e])
            even_p.append(rp)
            even_s.append(rs)
        else:
            o = l // 2
            mp, rp = odd_mixer_prompt(hp, w_in_odd[o], rel_bias[o], w_out_odd[o])
            ms, rs = odd_mixer_sample(hs, cache_c_k[o], cache_c_v[o], past_len, w_in_odd[o], rel_bias[o], w_out_odd[o])
            odd_p.append(rp)
            odd_s.append(rs)
        xp = xp + rmsnorm(mp, g_post_mix[l])
        xs = xs + rmsnorm(ms, g_post_mix[l])
        xp = xp + rmsnorm(squared_relu_mlp(rmsnorm(xp, g_pre_ffn[l]), w_ffn_up[l], w_ffn_down[l]), g_post_ffn[l])
        xs = xs + rmsnorm(squared_relu_mlp(rmsnorm(xs, g_pre_ffn[l]), w_ffn_up[l], w_ffn_down[l]), g_post_ffn[l])

    new_pa_k = jnp.stack([r[0] for r in even_p])
    new_pa_v = jnp.stack([r[1] for r in even_p])
    new_pb_k = jnp.stack([r[2] for r in even_p])
    new_pb_v = jnp.stack([r[3] for r in even_p])
    new_pb_logf = jnp.stack([r[4] for r in even_p])
    new_pc_k = jnp.stack([r[0] for r in odd_p])
    new_pc_v = jnp.stack([r[1] for r in odd_p])
    new_sa_k = jnp.stack([r[0] for r in even_s])
    new_sa_v = jnp.stack([r[1] for r in even_s])
    new_sb_k = jnp.stack([r[2] for r in even_s])
    new_sb_v = jnp.stack([r[3] for r in even_s])
    new_sb_logf = jnp.stack([r[4] for r in even_s])
    new_sc_k = jnp.stack([r[0] for r in odd_s])
    new_sc_v = jnp.stack([r[1] for r in odd_s])
    return (xp, xs, new_pa_k, new_pa_v, new_pb_k, new_pb_v, new_pb_logf, new_pc_k, new_pc_v,
            new_sa_k, new_sa_v, new_sb_k, new_sb_v, new_sb_logf, new_sc_k, new_sc_v)


_drawn_inputs = setup_inputs


def setup_inputs(seed=0):
    import zlib

    import numpy as np

    out = dict(_drawn_inputs(seed))
    spreads = {}
    factors = {}
    for name, (base, spread) in spreads.items():
        noise = np.random.default_rng([zlib.crc32(name.encode()), seed]).standard_normal(out[name].shape)
        drawn = base * np.exp(spread * noise) if base else spread * noise
        out[name] = __import__('jax').numpy.asarray(drawn.astype(out[name].dtype))
    for name, factor in factors.items():
        out[name] = (out[name] * factor).astype(out[name].dtype)
    return out
```

```python
import concourse.bass as bass
from concourse import mybir
from contextlib import ExitStack, contextmanager

P = 128
D_MODEL, D_FF = 1024, 4096
KT_D = D_MODEL // P
N_PROMPT, N_SAMPLE, N_CACHE = 1024, 64, 256
TOK = N_PROMPT + N_SAMPLE
CHUNKS = [(0, 384), (384, 384), (768, 320)]
GROUPS = 8
FF_GROUPS = 8
KCOLS = N_PROMPT + N_CACHE + N_SAMPLE
QCOLS = TOK + 64
C_BAND = 640
SAMPLE = 8
ORDER = [7, 6, 5, 4, 3, 2, 1, SAMPLE, 0]
S_AT = [24, 18, 12, 8, 4, 0, 0, 0, 0]
NEG = -1e30
EPS = 1e-6
LAM_INIT = 0.2
N_MM = 3 * KT_D


def block_of(kind, b):
    if b == SAMPLE:
        n = N_CACHE + N_SAMPLE
        return N_PROMPT, N_PROMPT, n, {"A": 1024 - 3 * P, "B": N_PROMPT, "C": C_BAND - 3 * P}[kind]
    n = P * (b + 1) if kind != "C" else min(C_BAND, P * (b + 1))
    k0 = P * (b + 1) - n
    return P * b, k0, n, {"A": 1024 - n, "B": k0, "C": C_BAND - n}[kind]


def key_tiles(kind, b):
    _, k0, n, _ = block_of(kind, b)
    first = SAMPLE if b == SAMPLE else k0 // P
    return [(o, min(P, n - o), first + o // P) for o in range(0, n, P)]


class Use:

    def __init__(self, what, block, m, tiles, engine):
        self.what, self.block, self.m, self.tiles, self.engine = what, block, m, tiles, engine


def bank_uses(kind):
    slots = [[] for _ in range(11)]
    for n, t in enumerate(([0, 1, 2], [3, 4, 5, 6], [7, SAMPLE + 2])):
        slots[0].append(Use("V", None, 0, t, "AD"[n % 2]))
    for s in range(1, 11):
        ot = [Use("OT", ORDER[s - 2], 0, [], "A")] if s >= 2 else []
        if s == 10:
            slots[s] += ot
        else:
            b = ORDER[s - 1]
            tiles = key_tiles(kind, b)
            n = 0
            for m in range(1 if kind == "A" else 2):
                for o in range(0, len(tiles), 4):
                    slots[s].append(Use("T", b, m, tiles[o:o + 4], "AD"[n % 2]))
                    n += 1
            slots[s] += ot + [Use("PV", b, 0, tiles, "D")]
    flat = [u for slot in slots for u in slot]
    count = {"A": 0, "D": 0}
    for n, u in enumerate(flat):
        u.n = n
        count[u.engine] += 1
        u.nth = count[u.engine]
        u.bank = n % 2
        u.prev = flat[n - 2] if n >= 2 else None
    return slots, flat, count


USES = {k: bank_uses(k) for k in "ABC"}


class Section:

    def __init__(self, kind, layer, reps, per, units=0, att="", g0=0, proj=False, f=0, last=False, nxt=0):
        self.kind, self.layer, self.reps, self.per = kind, layer, reps, per
        self.units = units
        self.att, self.g0, self.proj = att, g0, proj
        self.f, self.last, self.nxt = f, last, nxt
        self.base, self.unit, self.loaded = {}, 0, 0

    def at(self, i, name, k=0):
        v = self.base.get(name, 0) + k
        return v if self.reps == 1 else i * self.per.get(name, 0) + v

    def end(self, name):
        return self.base.get(name, 0) + self.per.get(name, 0) * self.reps

    def pick(self, i, first, per):
        return first if self.reps == 1 else i * per + first


STAGE = [0, 1, 2, 0]


def stage_loads(units):
    return {f"ld{s}": 16 * sum(STAGE[u] == s for u in units) for s in range(3)}


def add(*counts):
    out = {}
    for c in counts:
        for name, v in c.items():
            out[name] = out.get(name, 0) + v
    return out


FROM_ONE = ("S", "ttr", "xpe", "xA", "xD")


def make_sections():
    out = []
    triple, quad = stage_loads(range(3)), stage_loads(range(4))

    def attention(layer, kind, g0, reps, proj):
        _, flat, count = USES[kind]
        per = dict(qkhi=2, qklo=2, S=18, ttr=18, nm=18, ex=18, ri=9, xpe=len(flat), xA=count["A"], xD=count["D"],
                   bias=16 if kind == "A" else 32, vc=16, kst=16, vst=16)
        if kind == "A":
            per.update(cs=9, comb=9, ms=9, rs=9, on2=9)
        if kind == "C":
            per.update(cm=1)
        if proj:
            per = add(per, dict(D=9, evA=9, whi=3, wlo=3, kc=16, ost=16), triple)
        else:
            per = add(per, dict(whi=1, wlo=1, ld0=16, os0=64, os1=48, ohi=8, olo=8))
        out.append(Section("ATT", layer, reps, per, units=3 * proj, att=kind, g0=g0, proj=proj))

    for layer in (0, 1):
        n = 4 if layer == 0 else 3
        out.append(Section("T0", layer, 1, add(dict(D=3 * n, evA=3 * n, whi=3, wlo=3, kc=16), triple), units=n))
        if layer == 0:
            attention(0, "A", 0, 4, True)
            attention(0, "B", 4, 3, True)
            attention(0, "B", 7, 1, False)
        else:
            attention(1, "C", 8, 7, True)
            attention(1, "C", 15, 1, False)
        out.append(Section("OUT", layer, 1, add(dict(D=24, evA=24, whi=8, wlo=8), quad, quad), units=8))
        for f, reps in ((0, 1), (1, FF_GROUPS - 2), (FF_GROUPS - 1, 1)):
            last = f == FF_GROUPS - 1
            nxt = 4 if not last else 3 if layer == 0 else 0
            per = add(dict(D=36, evA=12, evD=24, uhi=12, um=12, uu=12, whi=4 + nxt, wlo=4 + nxt), quad, stage_loads(range(nxt)))
            out.append(Section("FF", layer, reps, per, units=8, f=f, last=last, nxt=nxt))
    base, unit, loaded = add(dict(whi=4, wlo=4), quad, {name: 1 for name in FROM_ONE}), 0, 4
    for s in out:
        s.base, s.unit, s.loaded = dict(base), unit, loaded
        unit += s.reps * s.units
        loaded += s.reps * s.per["wlo"]
        base = add(base, {name: v * s.reps for name, v in s.per.items()})
    assert base["wlo"] == unit == loaded
    return out, base, unit


SECTIONS, TOTALS, UNITS = make_sections()


def section(kind, layer, last=False):
    return next(s for s in SECTIONS if s.kind == kind and s.layer == layer and (not last or s.last))


NORMS = {0: dict(pre=("pre_mix", 0)), 1: dict(post=("post_mix", 0), pre=("pre_ffn", 0)),
         2: dict(post=("post_ffn", 0), pre=("pre_mix", 1)), 3: dict(post=("post_mix", 1), pre=("pre_ffn", 1)),
         4: dict(post=("post_ffn", 1))}
JOBS = [(n, c, part) for n in range(5) for c in range(3) for part in ("post", "pre") if part in NORMS[n]]
GAINS = [(which, layer) for which in ("pre_mix", "post_mix", "pre_ffn", "post_ffn") for layer in (0, 1)]


def nth_of(n, c, part):
    return [j for j in JOBS if j[2] == part].index((n, c, part))


PLAN = {
    "act": [(0, "post_sq"), (3, "pre_sq"), (6, "pre_hi")],
    "dve": [(0, "post_red"), (1, "post_diag"), (2, "post_x"), (3, "pre_red"), (4, "pre_diag"), (5, "pre_h"), (6, "pre_lo")],
    "pe": [(1, "post_stat"), (2, "post_bc"), (4, "pre_stat"), (5, "pre_bc")],
    "pool": [(0, "post_load"), (1, "post_pow"), (2, "post_x"), (4, "pre_pow"), (6, "pre_lo")],
}
LAST_TICK = 4 * 2 + 6


def norm_pieces(engine, n, tick):
    return [(c, what) for c in range(3) for at, what in PLAN[engine]
            if 4 * c + at == tick and what.split("_")[0] in NORMS[n]]


NORM_ON = 9


def build_program(nc, x_in, w_in, gains_in, subg_in, bf_in, lam_in, kcache, vcache, logf_cache, alibi, rel_bias,
                  ident_in, identb_in, tri_in, y_out, k_out, v_out, logf_out, vband_out):
    f32, f32r, bf16 = mybir.dt.float32, mybir.dt.float32r, mybir.dt.bfloat16
    ALU, ACT, AX = mybir.AluOpType, mybir.ActivationFunctionType, mybir.AxisListType
    ctx = ExitStack()
    with ctx:
        spot = [-(-nc.sbuf_base // 32) * 32]

        def place(name, offset, shape, dt=f32, size=4):
            for n in shape[1:]:
                size *= n
            assert offset + size <= nc.sbuf_usable_end, (name, offset, size)
            return nc.alloc_sbuf_tensor_at(name, shape, dt, offset=offset), offset + -(-size // 32) * 32

        def own(name, shape, dt=f32, size=4):
            t, spot[0] = place(name, spot[0], shape, dt, size)
            return t

        XH, XL = own("XH", [P, 8 * TOK], f32r), own("XL", [P, 8 * TOK], f32r)
        WH = [own(f"WH{s}", [P, 8 * P], f32r) for s in range(4)]
        WL = [own(f"WL{s}", [P, 8 * P], f32r) for s in range(4)]
        WS = [own(f"WS{s}", [P, 8 * P]) for s in range(3)]
        ident, ones = own("ident", [P, P]), own("ones", [P, P])
        identb, trib = own("identb", [P, P], bf16, 2), own("trib", [P, P], bf16, 2)
        G = own("G", [P, 8 * KT_D])
        subg, bF, nlam = own("subg", [P, 1]), own("bF", [8, 1]), own("nlam", [P, 1])
        halfpow = own("halfpow", [P, 3])
        ST, RS = own("ST", [P, 3]), own("RS", [P, 3])
        M, NM, L, RI = (own(n, [P, 4]) for n in ("M", "NM", "L", "RI"))
        CS, MS, RSO = (own(n, [P, 2]) for n in ("CS", "MS", "RSO"))
        hold = own("hold", [P, 1])

        r, xb = spot[0], 8 * TOK * 4
        XRES, _ = place("XRES", r, [P, 8 * TOK])
        U, _ = place("U", r, [P, 8 * TOK], f32r)
        ACC, z = place("ACC", r + xb, [P, 8 * TOK])
        QT, z1 = place("QT", z, [P, TOK])
        KT, z1 = place("KT", z1, [P, KCOLS])
        VT, z1 = place("VT", z1, [P, TOK])
        TU, z2 = place("TU", z, [P, 2, 384])
        TS, _ = place("TS", z2, [P, 2, 384])
        SQ, z1 = place("SQ", z1, [P, 4 * 384])
        PSa, z1 = place("PSa", z1, [P, 384])
        PSb, z1 = place("PSb", z1, [P, 384])
        DG, z1 = place("DG", z1, [P, 384])
        Qh, a = place("Qh", r, [P, QCOLS], f32r)
        Ql, a = place("Ql", a, [P, QCOLS], f32r)
        Kh, a = place("Kh", a, [P, KCOLS], f32r)
        Kl, a = place("Kl", a, [P, KCOLS], f32r)
        V, a = place("V", a, [P, 11, P])
        BIAS, a = place("BIAS", a, [P, 2, KCOLS])
        f0 = a
        PR, a = place("PR", a, [P, 2, 2, N_PROMPT])
        PT, a = place("PT", a, [P, 2, 8, P])
        OT, a = place("OT", a, [P, TOK])
        ON, a = place("ON", a, [P, P])
        assert a <= z
        ZF, f1 = place("ZF", f0, [8, KCOLS])
        FA, f1 = place("FA", f1, [8, KCOLS])
        LF, f1 = place("LF", f1, [8, KCOLS])
        NC, f1 = place("NC", f1, [8, KCOLS])
        ZZ, f1 = place("ZZ", f1, [8, KCOLS])
        LQ, f1 = place("LQ", f1, [P, 4, 64])
        LP, f1 = place("LP", f1, [P, 2])
        assert f1 <= z
        RB0, z3 = place("RB0", z, [16, 513])
        RB1, z3 = place("RB1", z3, [16, 768])

        x_scr = [nc.dram_tensor(f"x_scr{n}", (P, 8 * TOK), f32).ap() for n in range(3)]
        o_scr = nc.dram_tensor("o_scr", (GROUPS, P, TOK), f32).ap()
        nc_scr = nc.dram_tensor("nc_scr", (8, KCOLS), f32).ap()
        rel_t = nc.dram_tensor("rel_scr", (16, 768), f32)
        toep_scr = nc.dram_tensor("toep_scr", (16, P, C_BAND), f32).ap()

        ps = ctx.enter_context(nc.psum_tensor("ps", [P, 8, 512], f32))

        def semaphore(name):
            return ctx.enter_context(nc.semaphore("s_" + name))

        names = ("D evA evD "
                 "ld0 ld1 ld2 whi wlo "
                 "qkhi qklo kc vc kst vst bias cm "
                 "S ttr nm ex ri cs comb "
                 "xpe xA xD "
                 "ms rs on2 "
                 "ost os0 os1 ohi olo "
                 "uhi um uu").split()
        sem = {n: semaphore(n) for n in names}
        sem.update({n: semaphore(n) for n in (
            "xl0 xl1 xl2 xst0 xst1 xst2 "
            "sq red ps sta st pw dg rb xs xuD xuP hs hh hlD hlP az").split()})
        sem.update({n: semaphore(n) for n in "const pad ones fabs fexp flog fl flogf fscan fst lamdot lamexp lam rbias rel rels toep vb".split()})
        block = ctx.enter_context(nc.Block())

        def wait(eng, name, value):
            if not isinstance(value, int) or value > 0:
                eng.wait_ge(sem[name], value)

        @contextmanager
        def runs(eng, sec):
            if sec.reps == 1:
                yield None
            else:
                with eng.Fori(0, sec.reps, 1) as i:
                    yield i

        def ct(buf, c, k, n=1):
            o, w = CHUNKS[c]
            return buf[:, 8 * o + k * w:8 * o + (k + n) * w]

        def gain(which, k):
            j = KT_D * GAINS.index(which) + k
            return G[:, j:j + 1]

        def norms_over(eng, first_attention):
            n = 0 if first_attention.layer == 0 else 2
            for name in ("hh", "hlD", "hlP"):
                wait(eng, name, nth_of(n, 2, "pre") + 1)
            for c in range(3):
                wait(eng, f"xst{c}", 16 * n)
            wait(eng, "fst", 48)

        def transposed(use, bank):
            rows = [P if use.what == "V" and t != SAMPLE + 2 else N_SAMPLE if use.what == "V" else t[1] for t in use.tiles]
            first = use.tiles[0] if use.what == "V" else use.tiles[0][0] // P
            buf = V[:, :, :] if use.what == "V" else PT[:, use.m, :, :]
            full = sum(n == P for n in rows)
            out = []
            if full:
                out.append((buf[:, first:first + full, :].rearrange("p t q -> p (t q)"), bank[:, 0:full * P]))
            if full < len(rows):
                last = use.tiles[-1] if use.what == "V" else first + full
                out.append((buf[0:N_SAMPLE, last, :], bank[0:N_SAMPLE, full * P:(full + 1) * P]))
            return out

        @block.sync
        def _(sp):
            def load_unit(sec, i, k, u, prev):
                n = sec.pick(i, sec.loaded + k, sec.per["wlo"])
                wait(sp, "wlo", sec.pick(i, sec.loaded + k - prev + 1, sec.per["wlo"]))
                sp.dma_start(WS[STAGE[u]][:, :], w_in[n, :, :]).then_inc(sem[f"ld{STAGE[u]}"], 16)

            def load_quad(sec, i, k, units=4):
                for u in range(units):
                    load_unit(sec, i, k + u, u, (1, 4, 4, 3)[u])

            for u in range(3):
                sp.dma_start(WS[u][:, :], w_in[u, :, :]).then_inc(sem[f"ld{u}"], 16)
            sp.dma_start(RB0[:, :], rel_bias).then_inc(sem["rbias"], 16)
            for dst, src in ((ident, ident_in), (identb, identb_in), (trib, tri_in), (G, gains_in), (subg, subg_in), (bF, bf_in)):
                sp.dma_start(dst[:, :], src).then_inc(sem["const"], 16)
            sp.wait_ge(sem["wlo"], 1)
            sp.dma_start(WS[0][:, :], w_in[3, :, :]).then_inc(sem["ld0"], 16)
            sp.dma_start(vband_out, vcache[8:16, :, :, :]).then_inc(sem["vb"], 16)
            sp.wait_ge(sem["rel"], 3)
            sp.dma_start(rel_t.ap(), RB1[:, :]).then_inc(sem["rels"], 16)
            sp.wait_ge(sem["rels"], 16)
            sp.dma_start(toep_scr, bass.AP(rel_t, P - 1, [[768, 16], [-1, P], [1, C_BAND]])).then_inc(sem["toep"], 16)
            for sec in SECTIONS:
                if sec.kind == "T0":
                    wait(sp, "uu", sec.at(None, "uu"))
                    sp.dma_start(KT[:, N_PROMPT:N_PROMPT + N_CACHE], kcache[GROUPS * sec.layer, :, :]).then_inc(sem["kc"], 16)
                    for u in range(3):
                        load_unit(sec, None, u, u, (1, 4, 4)[u] if sec.layer == 0 else 3)
                    if sec.layer == 0:
                        sp.wait_ge(sem["D"], 10)
                        sp.dma_start(LF[:, N_PROMPT:N_PROMPT + N_CACHE], logf_cache).then_inc(sem["fl"], 16)
                        for k in range(4):
                            sp.dma_start(LQ[:, k, :], lam_in[k:k + 1, :].to_broadcast([P, 64])).then_inc(sem["fl"], 16)
                        sp.wait_ge(sem["flogf"], 2)
                        sp.dma_start(logf_out[:, 0:N_PROMPT], LF[:, 0:N_PROMPT]).then_inc(sem["fst"], 16)
                        sp.dma_start(logf_out[:, N_PROMPT:TOK], LF[:, N_PROMPT + N_CACHE:]).then_inc(sem["fst"], 16)
                        sp.wait_ge(sem["fscan"], 2)
                        sp.dma_start(nc_scr, NC[:, :]).then_inc(sem["fst"], 16)
                elif sec.kind == "ATT":
                    if sec.g0 % GROUPS == 0:
                        norms_over(sp, sec)
                        sp.wait_ge(sem["toep"], 16)
                    with runs(sp, sec) as i:
                        g = sec.pick(i, sec.g0, 1)
                        wait(sp, "ttr", sec.at(i, "ttr"))
                        if sec.att == "A":
                            sp.dma_start(BIAS[:, 0, 0:1024], alibi[g, :, :]).then_inc(sem["bias"], 16)
                        for m in range(2):
                            if sec.att == "B":
                                row = bass.AP(nc_scr.tensor, sec.pick(i, (2 * (sec.g0 - 4) + m) * KCOLS, 2 * KCOLS), [[0, P], [1, KCOLS]])
                                sp.dma_start(BIAS[:, m, :], row).then_inc(sem["bias"], 16)
                            elif sec.att == "C":
                                sp.dma_start(BIAS[:, m, 0:C_BAND], toep_scr[sec.pick(i, 2 * (sec.g0 - 8) + m, 2), :, :])\
                                    .then_inc(sem["bias"], 16)
                        wait(sp, "xpe", sec.at(i, "xpe"))
                        sp.dma_start(V[:, 8:10, :], vcache[g, :, :, :]).then_inc(sem["vc"], 16)
                        wait(sp, "evA", sec.at(i, "evA"))
                        sp.wait_ge(sem["kc"], sec.at(i, "kc"))
                        sp.dma_start(k_out[g, :, :], KT[:, :]).then_inc(sem["kst"], 16)
                        sp.dma_start(v_out[g, :, :], VT[:, :]).then_inc(sem["vst"], 16)
                        if sec.proj:
                            for u in range(3):
                                load_unit(sec, i, u, u, 3)
                            sp.wait_ge(sem["qkhi"], sec.at(i, "qkhi", 2))
                            sp.wait_ge(sem["qklo"], sec.at(i, "qklo", 2))
                            sp.wait_ge(sem["kst"], sec.at(i, "kst", 16))
                            sp.dma_start(KT[:, N_PROMPT:N_PROMPT + N_CACHE], kcache[sec.pick(i, sec.g0 + 1, 1), :, :])\
                                .then_inc(sem["kc"], 16)
                            sp.wait_ge(sem["xA"], sec.at(i, "xA", sec.per["xA"]))
                            sp.dma_start(o_scr[sec.pick(i, sec.g0 % GROUPS, 1), :, :], OT[:, :]).then_inc(sem["ost"], 16)
                        else:
                            load_unit(sec, i, 0, 3, 3)
                            for o in range(7):
                                sp.wait_ge(sem["ost"], sec.at(i, "ost"))
                                if o == 0:
                                    sp.wait_ge(sem["qklo"], sec.at(i, "qklo", 1))
                                elif o == 1:
                                    sp.wait_ge(sem["vst"], sec.at(i, "vst", 16))
                                    sp.wait_ge(sem["xpe"], sec.at(i, "xpe", 3))
                                else:
                                    sp.wait_ge(sem["olo"], sec.at(i, "olo", o - 1))
                                sp.dma_start((QT, VT)[o % 2][:, :], o_scr[o, :, :]).then_inc(sem[f"os{o % 2}"], 16)
                elif sec.kind == "OUT":
                    load_quad(sec, None, 0)
                    load_quad(sec, None, 4)
                else:
                    with runs(sp, sec) as i:
                        load_quad(sec, i, 0)
                        load_quad(sec, i, 4, sec.nxt)
            for name in ("kst", "vst", "ost"):
                sp.wait_ge(sem[name], TOTALS[name])
            sp.wait_ge(sem["fst"], 48)
            sp.wait_ge(sem["toep"], 16)
            sp.wait_ge(sem["vb"], 16)
            for c in range(3):
                sp.wait_ge(sem[f"xst{c}"], 64)

        @block.gpsimd
        def _(pool):
            def lo_unit(sec, i, k, u):
                pool.wait_ge(sem["whi"], sec.pick(i, sec.loaded + k + 1, sec.per["wlo"]))
                pool.tensor_tensor(WL[u][:, :], WS[STAGE[u]][:, :], WH[u][:, :].bitcast(f32), ALU.subtract)\
                    .then_inc(sem["wlo"], 1)

            def norm(n, c, what):
                o, w = CHUNKS[c]
                cols = slice(8 * o, 8 * (o + w))
                if what == "post_load" and n in (2, 4):
                    pool.wait_ge(sem["D"], section("FF", n // 2 - 1, True).at(None, "D", 12 + 8 * (c + 1)))
                    pool.wait_ge(sem[f"xst{c}"], 16 * (n - 1))
                    pool.dma_start(ct(XRES, c, 0, 8), x_scr[n - 2][:, cols]).then_inc(sem[f"xl{c}"], 16)
                elif what in ("post_pow", "pre_pow"):
                    j = JOBS.index((n, c, what[:-4]))
                    pool.wait_ge(sem["st"], j + 1)
                    full = w // P
                    ins = pool.tensor_tensor(RS[:, 0:full], ST[:, 0:full], halfpow[:, 0:full], ALU.pow)
                    if w % P:
                        h = w % P
                        ins = pool.tensor_tensor(RS[0:h, full:full + 1], ST[0:h, full:full + 1], halfpow[0:h, 0:1], ALU.pow)
                    ins.then_inc(sem["pw"], 1)
                elif what == "post_x":
                    j = nth_of(n, c, "post")
                    pool.wait_ge(sem["xs"], j + 1)
                    pool.wait_ge(sem[f"xl{c}"], 16 * (n + 1))
                    pool.tensor_tensor(ct(XRES, c, 5, 3), ct(XRES, c, 5, 3), ct(ACC, c, 5, 3), ALU.add).then_inc(sem["xuP"], 1)
                    pool.wait_ge(sem["xuP"], j + 1)
                    pool.wait_ge(sem["xuD"], j + 1)
                    dst = y_out if n == 4 else x_scr[n - 1]
                    pool.dma_start(dst[:, cols], ct(XRES, c, 0, 8)).then_inc(sem[f"xst{c}"], 16)
                elif what == "pre_lo":
                    j = nth_of(n, c, "pre")
                    pool.wait_ge(sem["hh"], j + 1)
                    pool.tensor_tensor(ct(XL, c, 4, 4), ct(ACC, c, 4, 4), ct(XH, c, 4, 4).bitcast(f32), ALU.subtract)\
                        .then_inc(sem["hlP"], 1)
                    if n in (1, 3):
                        pool.wait_ge(sem["hlP"], j + 1)
                        pool.wait_ge(sem["hlD"], j + 1)
                        pool.memset(ct(ACC, c, 0, 8), 0.0).then_inc(sem["az"], 1)

            def norm_at(n, tick):
                for c, what in norm_pieces("pool", n, tick):
                    norm(n, c, what)

            first = Section("START", 0, 1, dict(wlo=4))
            for c, (o, w) in enumerate(CHUNKS):
                pool.dma_start(ct(XRES, c, 0, 8), x_in[:, 8 * o:8 * (o + w)]).then_inc(sem[f"xl{c}"], 16)
            pool.memset(ones[:, :], 1.0).then_inc(sem["ones"], 1)
            pool.memset(halfpow[:, :], -0.5).then_inc(sem["ones"], 1)
            pool.wait_ge(sem["ones"], 2)
            lo_unit(first, None, 0, 0)
            for c in range(3):
                norm(0, c, "pre_pow")
                norm(0, c, "pre_lo")
                if c == 0:
                    for u in (1, 2, 3):
                        lo_unit(first, None, u, u)
            for sec in SECTIONS:
                if sec.kind == "T0":
                    for s in range(9):
                        if s >= 6:
                            lo_unit(sec, None, s - 6, s - 6)
                        if sec.layer == 1:
                            norm_at(2, NORM_ON + s)
                elif sec.kind == "ATT":
                    if sec.g0 % GROUPS == 0:
                        norms_over(pool, sec)
                        pool.memset(Qh[:, TOK:QCOLS].bitcast(f32), 0.0).then_inc(sem["pad"], 1)
                        pool.memset(Ql[:, TOK:QCOLS].bitcast(f32), 0.0).then_inc(sem["pad"], 1)
                    with runs(pool, sec) as i:
                        def rstd(k):
                            q = k % 2
                            pool.wait_ge(sem["ms"], sec.at(i, "ms", k + 1))
                            pool.tensor_tensor(RSO[:, q:q + 1], MS[:, q:q + 1], halfpow[:, 0:1], ALU.pow)\
                                .then_inc(sem["rs"], 1)

                        for s in range(9):
                            if sec.att == "A" and s >= 1:
                                rstd(s - 1)
                            if sec.proj and s >= 6:
                                lo_unit(sec, i, s - 6, s - 6)
                        if sec.att == "A":
                            rstd(8)
                        if not sec.proj:
                            lo_unit(sec, i, 0, 3)
                            for o in range(8):
                                pool.wait_ge(sem["ohi"], sec.at(i, "ohi", o + 1))
                                src = (QT, VT)[o % 2] if o < 7 else OT
                                for c, (t0, w) in enumerate(CHUNKS):
                                    ins = pool.tensor_tensor(ct(XL, c, o), src[:, t0:t0 + w], ct(XH, c, o).bitcast(f32), ALU.subtract)
                                ins.then_inc(sem["olo"], 1)
                elif sec.kind == "OUT":
                    n = 1 + 2 * sec.layer
                    pool.wait_ge(sem["D"], sec.at(None, "D", 1))
                    for c, (t0, w) in enumerate(CHUNKS):
                        if n == 3:
                            pool.wait_ge(sem[f"xst{c}"], 32)
                        src = x_in if n == 1 else x_scr[1]
                        pool.dma_start(ct(XRES, c, 0, 8), src[:, 8 * t0:8 * (t0 + w)]).then_inc(sem[f"xl{c}"], 16)
                    for t in range(24):
                        if t % 12 >= 8:
                            lo_unit(sec, None, 4 * (t // 12) + t % 4, t % 4)
                        norm_at(n, t - 15)
                else:
                    with runs(pool, sec) as i:
                        for t in range(12):
                            if t >= 8:
                                lo_unit(sec, i, t - 8, t - 8)
                            if sec.f == 0:
                                norm_at(1 + 2 * sec.layer, NORM_ON + t)
                        for t in range(12):
                            if t >= 8 and t - 8 < sec.nxt:
                                lo_unit(sec, i, 4 + t - 8, t - 8)
                            if sec.last:
                                norm_at(2 + 2 * sec.layer, t - 3)
                    if sec.last and sec.layer == 1:
                        for tick in range(NORM_ON, LAST_TICK + 1):
                            norm_at(4, tick)

        @block.scalar
        def _(act):
            def hi_unit(sec, i, k, u, uses, release):
                st = STAGE[u]
                act.wait_ge(sem[f"ld{st}"], sec.at(i, f"ld{st}", 16 * uses))
                wait(act, "D", release)
                act.copy(WH[u][:, :], WS[st][:, :]).then_inc(sem["whi"], 1)

            def norm(n, c, what):
                w = CHUNKS[c][1]
                if what in ("post_sq", "pre_sq"):
                    part = what[:-3]
                    j = JOBS.index((n, c, part))
                    if part == "pre":
                        if n == 0:
                            act.wait_ge(sem[f"xl{c}"], 16)
                        else:
                            act.wait_ge(sem["xuD"], nth_of(n, c, "post") + 1)
                            act.wait_ge(sem["xuP"], nth_of(n, c, "post") + 1)
                    elif n in (1, 3):
                        act.wait_ge(sem["evA"], section("OUT", n // 2).at(None, "evA", 12 + 4 * (c + 1)))
                    else:
                        act.wait_ge(sem["evD"], section("FF", n // 2 - 1, True).at(None, "evD", 8 * (c + 1)))
                    for h in range(2):
                        wait(act, "red", 2 * j + h)
                        act.activation(SQ[:, 0:4 * w], ct(ACC if part == "post" else XRES, c, 4 * h, 4), ACT.Square)\
                            .then_inc(sem["sq"], 1)
                elif what == "pre_hi":
                    act.wait_ge(sem["hs"], nth_of(n, c, "pre") + 1)
                    act.copy(ct(XH, c, 0, 8), ct(ACC, c, 0, 8)).then_inc(sem["hh"], 1)

            def norm_at(n, tick):
                for c, what in norm_pieces("act", n, tick):
                    norm(n, c, what)

            def empty_qkv(s, bank):
                c, u = s // 3, s % 3
                t0, w = CHUNKS[c]
                if u == 0:
                    act.activation(QT[:, t0:t0 + w], bank[:, 0:w], ACT.Copy, scale=0.125).then_inc(sem["evA"], 1)
                elif u == 1 and c < 2:
                    act.copy(KT[:, t0:t0 + w], bank[:, 0:w]).then_inc(sem["evA"], 1)
                elif u == 1:
                    act.copy(KT[:, t0:N_PROMPT], bank[:, 0:N_PROMPT - t0])
                    act.copy(KT[:, N_PROMPT + N_CACHE:], bank[:, N_PROMPT - t0:w]).then_inc(sem["evA"], 1)
                else:
                    act.copy(VT[:, t0:t0 + w], bank[:, 0:w]).then_inc(sem["evA"], 1)

            first = Section("START", 0, 1, {})
            act.nop().then_inc(sem["xA"], 1)
            for u in range(3):
                hi_unit(first, None, u, u, 1, 0)
            for c in range(3):
                norm(0, c, "pre_sq")
                norm(0, c, "pre_hi")
                if c == 0:
                    hi_unit(first, None, 3, 3, 2, 0)
            act.wait_ge(sem["rbias"], 16)
            act.copy(RB1[:, 383:767], RB0[:, 129:513][:, ::-1]).then_inc(sem["rel"], 1)
            act.copy(RB1[:, 767:768], RB0[:, 128:129]).then_inc(sem["rel"], 1)
            act.copy(RB1[:, 0:383], RB0[:, 512:513].to_broadcast([16, 383])).then_inc(sem["rel"], 1)
            act.wait_ge(sem["const"], 96)
            act.wait_ge(sem["rels"], 16)
            for sec in SECTIONS:
                if sec.kind == "T0":
                    for s in range(9):
                        act.wait_ge(sem["D"], sec.at(None, "D", s + 1))
                        empty_qkv(s, ps[:, s % 2, :])
                        if s >= 6:
                            hi_unit(sec, None, s - 6, s - 6, 1, sec.at(None, "D", s + 1))
                        if sec.layer == 1:
                            norm_at(2, NORM_ON + s)
                    if sec.layer == 0:
                        for c, (t0, w) in enumerate(CHUNKS):
                            act.wait_ge(sem["D"], 10 + c)
                            act.activation(ZF[:, t0:t0 + w], ps[0:8, (9 + c) % 2, 0:w], ACT.Identity, bias=bF[:, 0:1])\
                                .then_inc(sem["evA"], 1)
                        act.wait_ge(sem["lamdot"], 2)
                        act.activation(LP[:, :], LP[:, :], ACT.Exp).then_inc(sem["lamexp"], 1)
                        act.wait_ge(sem["fabs"], 1)
                        act.activation(FA[:, 0:TOK], FA[:, 0:TOK], ACT.Exp, scale=-1.0).then_inc(sem["fexp"], 1)
                        act.wait_ge(sem["fexp"], 1)
                        act.activation(FA[:, 0:TOK], FA[:, 0:TOK], ACT.Ln, bias=1.0).then_inc(sem["flog"], 1)
                elif sec.kind == "ATT":
                    kind = sec.att
                    if sec.g0 % GROUPS == 0:
                        norms_over(act, sec)
                        act.wait_ge(sem["lam"], 1)
                    with runs(act, sec) as i:
                        def empty(use):
                            act.wait_ge(sem["xpe"], sec.at(i, "xpe", use.n + 1))
                            bank = ps[:, 6 + use.bank, :]
                            if use.what == "OT":
                                q0 = block_of(kind, use.block)[0]
                                w = N_SAMPLE if use.block == SAMPLE else P
                                if kind == "A":
                                    act.activation(OT[:, q0:q0 + w], bank[:, 0:w], ACT.Copy, scale=subg[:, 0:1]).then_inc(sem["xA"], 1)
                                else:
                                    act.copy(OT[:, q0:q0 + w], bank[:, 0:w]).then_inc(sem["xA"], 1)
                                return
                            for dst, src in transposed(use, bank):
                                ins = act.copy(dst, src)
                            ins.then_inc(sem["xA"], 1)

                        def exps(s, m):
                            n, q = block_of(kind, ORDER[s])[2], 2 * (s % 2) + m
                            act.wait_ge(sem["nm"], sec.at(i, "nm", 2 * s + m + 1))
                            act.activation(PR[:, s % 2, m, 0:n], PR[:, s % 2, m, 0:n], ACT.Exp, bias=NM[:, q:q + 1],
                                           accum_out=L[:, q:q + 1]).then_inc(sem["ex"], 1)

                        def empty_dense(s):
                            u = s % 3
                            act.wait_ge(sem["D"], sec.at(i, "D", s + 1))
                            if u == 0:
                                act.wait_ge(sem["qklo"], sec.at(i, "qklo", 1))
                            elif u == 1:
                                act.wait_ge(sem["qklo"], sec.at(i, "qklo", 2))
                                act.wait_ge(sem["kst"], sec.at(i, "kst", 16))
                            else:
                                act.wait_ge(sem["vst"], sec.at(i, "vst", 16))
                                act.wait_ge(sem["xpe"], sec.at(i, "xpe", 3))
                            empty_qkv(s, ps[:, s % 2, :])

                        def output_hi(o):
                            if o < 7:
                                act.wait_ge(sem[f"os{o % 2}"], sec.at(i, f"os{o % 2}", 16 * (o // 2 + 1)))
                            else:
                                act.wait_ge(sem["xA"], sec.at(i, "xA", sec.per["xA"]))
                            act.wait_ge(sem["D"], sec.at(i, "D"))
                            src = (QT, VT)[o % 2] if o < 7 else OT
                            for c, (t0, w) in enumerate(CHUNKS):
                                ins = act.copy(ct(XH, c, o), src[:, t0:t0 + w])
                            ins.then_inc(sem["ohi"], 1)

                        wait(act, "S", sec.at(i, "S"))
                        act.wait_ge(sem["evA"], sec.at(i, "evA"))
                        act.copy(Qh[:, 0:TOK], QT[:, :]).then_inc(sem["qkhi"], 1)
                        act.wait_ge(sem["kc"], sec.at(i, "kc"))
                        act.copy(Kh[:, :], KT[:, :]).then_inc(sem["qkhi"], 1)
                        if not sec.proj:
                            hi_unit(sec, i, 0, 3, 1, 0)
                        for s in range(11):
                            mine = [use for use in USES[kind][0][s] if use.engine == "A"]
                            ts = [use for use in mine if use.what != "OT"]
                            ots = [use for use in mine if use.what == "OT"]
                            early = 0 < s < 9 and S_AT[s] < 12
                            if early:
                                exps(s, 0)
                                for use in ts[:1]:
                                    empty(use)
                                exps(s, 1)
                                ts = ts[1:]
                            for use in ts:
                                empty(use)
                            if s < 9 and not early:
                                exps(s, 0)
                                exps(s, 1)
                            for use in ots:
                                empty(use)
                            if sec.proj and s < 9:
                                empty_dense(s)
                                if s >= 6:
                                    hi_unit(sec, i, s - 6, s - 6, 1, sec.at(i, "D", s + 1))
                            if not sec.proj and 1 <= s < 8:
                                output_hi(s - 1)
                        if not sec.proj:
                            output_hi(7)
                elif sec.kind == "OUT":
                    for t in range(24):
                        q, c, u = t // 12, t % 12 // 4, t % 4
                        w = CHUNKS[c][1]
                        act.wait_ge(sem["D"], sec.at(None, "D", t + 1))
                        act.copy(ct(ACC, c, 4 * q + u), ps[:, t % 6, 0:w]).then_inc(sem["evA"], 1)
                        if c == 2:
                            uses = (2 if STAGE[u] == 0 else 1) * q + (2 if u == 3 else 1)
                            hi_unit(sec, None, 4 * q + u, u, uses, sec.at(None, "D", t + 1))
                        norm_at(1 + 2 * sec.layer, t - 15)
                else:
                    with runs(act, sec) as i:
                        for t in range(12):
                            c, u = t // 4, t % 4
                            w = CHUNKS[c][1]
                            act.wait_ge(sem["D"], sec.at(i, "D", t + 1))
                            if t >= 2 or sec.base.get("um", 0):
                                act.wait_ge(sem["um"], sec.at(i, "um", t - 1))
                            act.activation(TU[:, t % 2, 0:w], ps[:, t % 6, 0:w], ACT.Relu).then_inc(sem["evA"], 1)
                            act.wait_ge(sem["evA"], sec.at(i, "evA", t + 1))
                            if sec.f == 0:
                                act.wait_ge(sem[f"xst{c}"], 16 * (1 + 2 * sec.layer))
                            act.activation(ct(U, c, u), TU[:, t % 2, 0:w], ACT.Square).then_inc(sem["uhi"], 1)
                            if c == 2:
                                hi_unit(sec, i, u, u, 2 if u == 3 else 1, sec.at(i, "D", t + 1))
                            if sec.f == 0:
                                norm_at(1 + 2 * sec.layer, NORM_ON + t)
                        for t in range(12):
                            u = t % 4
                            if t >= 8 and u < sec.nxt:
                                uses = {0: 3, 3: 4}.get(u, 2)
                                hi_unit(sec, i, 4 + u, u, uses, sec.at(i, "D", 12 + 2 * (t + 1)))
                            if sec.last:
                                norm_at(2 + 2 * sec.layer, t - 3)
                    if sec.last and sec.layer == 1:
                        for tick in range(NORM_ON, LAST_TICK + 1):
                            norm_at(4, tick)

        @block.vector
        def _(dve):
            def norm(n, c, what):
                part, step = what.split("_")
                w = CHUNKS[c][1]
                j = JOBS.index((n, c, "pre" if step == "lo" else part))
                if step == "red":
                    wait(dve, "sta", j)
                    for h, buf in enumerate((PSa, PSb)):
                        dve.wait_ge(sem["sq"], 2 * j + h + 1)
                        dve.tensor_reduce(buf[:, 0:w], SQ[:, 0:4 * w].rearrange("p (k w) -> p w k", k=4), AX.X, ALU.add)\
                            .then_inc(sem["red"], 1)
                    dve.wait_ge(sem["red"], 2 * j + 2)
                    dve.tensor_tensor(PSa[:, 0:w], PSa[:, 0:w], PSb[:, 0:w], ALU.add).then_inc(sem["ps"], 1)
                elif step == "diag":
                    full, h = w // P, w % P
                    dve.wait_ge(sem["sta"], j + 1)
                    wait(dve, "pw", j)
                    ins = dve.tensor_scalar(ST[:, 0:full], ps[:, 6, 0:full], 1.0 / D_MODEL, EPS, ALU.mult, ALU.add)
                    if h:
                        ins = dve.tensor_scalar(ST[0:h, full:full + 1], ps[0:h, 6, full:full + 1], 1.0 / D_MODEL, EPS, ALU.mult, ALU.add)
                    ins.then_inc(sem["st"], 1)
                    dve.wait_ge(sem["pw"], j + 1)
                    wait(dve, "rb", j)
                    for q in range(full + (h > 0)):
                        v = P if q < full else h
                        ins = dve.tensor_scalar(DG[0:v, q * P:q * P + v], ident[0:v, 0:v], RS[0:v, q:q + 1], None, ALU.mult)
                    ins.then_inc(sem["dg"], 1)
                elif step in ("x", "h"):
                    src = ACC if step == "x" else XRES
                    dve.wait_ge(sem["rb"], j + 1)
                    if step == "h" and n:
                        dve.wait_ge(sem["xuP"], nth_of(n, c, "post") + 1)
                        dve.wait_ge(sem["xuD"], nth_of(n, c, "post") + 1)
                    for k in range(KT_D):
                        ins = dve.scalar_tensor_tensor(out=ct(ACC, c, k), in0=ct(src, c, k), scalar=gain(NORMS[n][part], k),
                                                       in1=ps[:, 7, 0:w], op0=ALU.mult, op1=ALU.mult)
                    if step == "h":
                        ins.then_inc(sem["hs"], 1)
                    else:
                        ins.then_inc(sem["xs"], 1)
                        dve.wait_ge(sem["xs"], nth_of(n, c, "post") + 1)
                        dve.wait_ge(sem[f"xl{c}"], 16 * (n + 1))
                        dve.tensor_tensor(ct(XRES, c, 0, 5), ct(XRES, c, 0, 5), ct(ACC, c, 0, 5), ALU.add).then_inc(sem["xuD"], 1)
                elif step == "lo":
                    dve.wait_ge(sem["hh"], nth_of(n, c, "pre") + 1)
                    dve.tensor_tensor(ct(XL, c, 0, 4), ct(ACC, c, 0, 4), ct(XH, c, 0, 4).bitcast(f32), ALU.subtract)\
                        .then_inc(sem["hlD"], 1)

            def norm_at(n, tick):
                for c, what in norm_pieces("dve", n, tick):
                    norm(n, c, what)

            for name in ("ttr", "xD"):
                dve.nop().then_inc(sem[name], 1)
            dve.wait_ge(sem["const"], 96)
            dve.tensor_scalar(subg[:, :], subg[:, :], 1.0 - LAM_INIT, None, ALU.mult).then_inc(sem["lam"], 1)
            for c in range(3):
                for what in ("pre_red", "pre_diag", "pre_h", "pre_lo"):
                    norm(0, c, what)
            for sec in SECTIONS:
                if sec.kind == "T0" and sec.layer == 0:
                    dve.wait_ge(sem["fl"], 80)
                    for k in range(2):
                        dve.tensor_tensor_reduce(out=LQ[:, 2 * k, :], in0=LQ[:, 2 * k, :], in1=LQ[:, 2 * k + 1, :],
                                                 scale=1.0, scalar=0.0, op0=ALU.mult, op1=ALU.add,
                                                 accum_out=LP[:, k:k + 1]).then_inc(sem["lamdot"], 1)
                    dve.wait_ge(sem["evA"], 12)
                    dve.scalar_tensor_tensor(out=FA[:, 0:TOK], in0=ZF[:, 0:TOK], scalar=-1.0, in1=ZF[:, 0:TOK],
                                             op0=ALU.mult, op1=ALU.max).then_inc(sem["fabs"], 1)
                    dve.memset(ZZ[:, :], 0.0).then_inc(sem["fabs"], 1)
                    dve.wait_ge(sem["lamexp"], 1)
                    dve.tensor_tensor(nlam[:, :], LP[:, 1:2], LP[:, 0:1], ALU.subtract).then_inc(sem["lam"], 1)
                    dve.wait_ge(sem["lam"], 2)
                    dve.tensor_scalar(nlam[:, :], nlam[:, :], -LAM_INIT, None, ALU.add).then_inc(sem["lam"], 1)
                    dve.wait_ge(sem["flog"], 1)
                    for t0, t1, to in ((0, N_PROMPT, 0), (N_PROMPT, TOK, N_PROMPT + N_CACHE)):
                        dve.scalar_tensor_tensor(out=LF[:, to:to + t1 - t0], in0=ZF[:, t0:t1], scalar=0.0, in1=FA[:, t0:t1],
                                                 op0=ALU.min, op1=ALU.subtract).then_inc(sem["flogf"], 1)
                    dve.wait_ge(sem["flogf"], 2)
                    dve.wait_ge(sem["fabs"], 2)
                    for t0, t1 in ((0, N_PROMPT), (N_PROMPT, KCOLS)):
                        dve.tensor_tensor_scan(NC[:, t0:t1], ZZ[:, t0:t1], LF[:, t0:t1], 0.0, ALU.add, ALU.subtract)\
                            .then_inc(sem["fscan"], 1)
                elif sec.kind == "T0":
                    for tick in range(NORM_ON, LAST_TICK + 1):
                        norm_at(2, tick)
                elif sec.kind == "ATT":
                    kind = sec.att
                    if sec.g0 % GROUPS == 0:
                        norms_over(dve, sec)
                        if sec.layer == 0:
                            dve.wait_ge(sem["lam"], 3)
                    with runs(dve, sec) as i:
                        def scores(s, m):
                            _, _, n, b0 = block_of(kind, ORDER[s])
                            q = 2 * (s % 2) + m
                            dve.wait_ge(sem["S"], sec.at(i, "S", 2 * s + m + 1))
                            dve.memset(hold[:, :], 0.0)
                            dve.tensor_tensor_reduce(
                                out=PR[:, s % 2, m, 0:n], in0=ps[:, 2 + 2 * m:4 + 2 * m, :].rearrange("p b n -> p (b n)")[:, 0:n],
                                in1=BIAS[:, 0 if kind == "A" else m, b0:b0 + n], scale=1.0, scalar=-3.0e38,
                                op0=ALU.add, op1=ALU.max, accum_out=M[:, q:q + 1]).then_inc(sem["ttr"], 1)
                            dve.wait_ge(sem["ttr"], sec.at(i, "ttr", 2 * s + m + 1))
                            dve.tensor_scalar(NM[:, q:q + 1], M[:, q:q + 1], -1.0, None, ALU.mult).then_inc(sem["nm"], 1)

                        def set_free(s):
                            if s < 2:
                                wait(dve, "xpe", sec.at(i, "xpe"))
                            else:
                                last = [use for use in USES[kind][1] if use.what == "T" and use.block == ORDER[s - 2]][-1]
                                dve.wait_ge(sem["xpe"], sec.at(i, "xpe", last.n + 1))

                        def empty(use, s):
                            dve.wait_ge(sem["xpe"], sec.at(i, "xpe", use.n + 1))
                            bank = ps[:, 6 + use.bank, :]
                            if use.what != "PV":
                                for dst, src in transposed(use, bank):
                                    ins = dve.tensor_copy(dst, src)
                                ins.then_inc(sem["xD"], 1)
                                return
                            k, q = s - 1, 2 * ((s - 1) % 2)
                            dve.wait_ge(sem["ri"], sec.at(i, "ri", k + 1))
                            if kind != "A":
                                dve.tensor_scalar(ON[:, 0:64], bank[:, 0:64], RI[:, q:q + 1], None, ALU.mult)
                                dve.tensor_scalar(ON[:, 64:P], bank[:, 64:P], RI[:, q + 1:q + 2], None, ALU.mult).then_inc(sem["xD"], 1)
                                return
                            dve.tensor_scalar(ON[:, :], bank[:, 0:P], RI[:, q:q + 1], None, ALU.mult).then_inc(sem["xD"], 1)
                            dve.wait_ge(sem["xD"], sec.at(i, "xD", use.nth))
                            dve.tensor_tensor_reduce(out=SQ[:, 0:P], in0=ON[:, :], in1=ON[:, :], scale=1.0 / P, scalar=EPS,
                                                     op0=ALU.mult, op1=ALU.add, accum_out=MS[:, k % 2:k % 2 + 1]).then_inc(sem["ms"], 1)

                        def sums(s):
                            q, n = 2 * (s % 2), block_of(kind, ORDER[s])[2]
                            dve.wait_ge(sem["ex"], sec.at(i, "ex", 2 * s + 2))
                            dve.reciprocal(RI[:, q:q + 2], L[:, q:q + 2]).then_inc(sem["ri"], 1)
                            if kind == "A":
                                dve.wait_ge(sem["ri"], sec.at(i, "ri", s + 1))
                                dve.scalar_tensor_tensor(out=CS[:, s % 2:s % 2 + 1], in0=L[:, q:q + 1], scalar=RI[:, q + 1:q + 2],
                                                         in1=nlam[:, 0:1], op0=ALU.mult, op1=ALU.mult).then_inc(sem["cs"], 1)
                                dve.wait_ge(sem["cs"], sec.at(i, "cs", s + 1))
                                dve.scalar_tensor_tensor(out=PR[:, s % 2, 0, 0:n], in0=PR[:, s % 2, 1, 0:n], scalar=CS[:, s % 2:s % 2 + 1],
                                                         in1=PR[:, s % 2, 0, 0:n], op0=ALU.mult, op1=ALU.add).then_inc(sem["comb"], 1)

                        def normed(k):
                            dve.wait_ge(sem["rs"], sec.at(i, "rs", k + 1))
                            dve.tensor_scalar(ON[:, :], ON[:, :], RSO[:, k % 2:k % 2 + 1], None, ALU.mult).then_inc(sem["on2"], 1)

                        dve.wait_ge(sem["qkhi"], sec.at(i, "qkhi", 1))
                        dve.tensor_tensor(Ql[:, 0:TOK], QT[:, :], Qh[:, 0:TOK].bitcast(f32), ALU.subtract).then_inc(sem["qklo"], 1)
                        dve.wait_ge(sem["qkhi"], sec.at(i, "qkhi", 2))
                        dve.tensor_tensor(Kl[:, :], KT[:, :], Kh[:, :].bitcast(f32), ALU.subtract).then_inc(sem["qklo"], 1)
                        dve.wait_ge(sem["bias"], sec.at(i, "bias", sec.per["bias"]))
                        if kind == "C":
                            for m in range(2):
                                dve.memset(BIAS[0:64, m, C_BAND - 64:C_BAND], NEG)
                                ins = dve.memset(BIAS[64:P, m, 0:64], NEG)
                            ins.then_inc(sem["cm"], 1)
                            dve.wait_ge(sem["cm"], sec.at(i, "cm", 1))
                        for s in range(11):
                            mine = [use for use in USES[kind][0][s] if use.engine == "D"]
                            early = 0 < s < 9 and S_AT[s] < 12
                            if early:
                                set_free(s)
                                scores(s, 0)
                                scores(s, 1)
                            for use in mine:
                                if use.what != "PV":
                                    empty(use, s)
                            if s < 9 and not early:
                                set_free(s)
                                scores(s, 0)
                                scores(s, 1)
                            for use in mine:
                                if use.what == "PV":
                                    empty(use, s)
                            if s < 9:
                                sums(s)
                            if kind == "A" and 1 <= s <= 9:
                                normed(s - 1)
                elif sec.kind == "OUT":
                    for t in range(24):
                        norm_at(1 + 2 * sec.layer, t - 15)
                elif sec.kind == "FF":
                    with runs(dve, sec) as i:
                        for t in range(12):
                            c, u = t // 4, t % 4
                            w = CHUNKS[c][1]
                            dve.wait_ge(sem["evA"], sec.at(i, "evA", t + 1))
                            dve.tensor_tensor(TS[:, t % 2, 0:w], TU[:, t % 2, 0:w], TU[:, t % 2, 0:w], ALU.mult).then_inc(sem["um"], 1)
                            dve.wait_ge(sem["um"], sec.at(i, "um", t + 1))
                            dve.wait_ge(sem["uhi"], sec.at(i, "uhi", t + 1))
                            dve.tensor_tensor(ct(U, c, 4 + u), TS[:, t % 2, 0:w], ct(U, c, u).bitcast(f32), ALU.subtract)\
                                .then_inc(sem["uu"], 1)
                            if sec.f == 0:
                                norm_at(1 + 2 * sec.layer, NORM_ON + t)
                        for t in range(12):
                            c, u = t // 4, t % 4
                            w = CHUNKS[c][1]
                            for v in (2 * t, 2 * t + 1):
                                dve.wait_ge(sem["D"], sec.at(i, "D", 12 + v + 1))
                                if sec.f == 0:
                                    dve.wait_ge(sem["az"], 3 * sec.layer + c + 1)
                                else:
                                    dve.wait_ge(sem["evD"], sec.at(i, "evD", v + 1 - 24))
                                acc = ct(ACC, c, 2 * u + v % 2)
                                dve.tensor_tensor(acc, ps[:, v % 6, 0:w], acc, ALU.add).then_inc(sem["evD"], 1)
                            if sec.last:
                                norm_at(2 + 2 * sec.layer, t - 3)
                    if sec.last and sec.layer == 1:
                        for tick in range(NORM_ON, LAST_TICK + 1):
                            norm_at(4, tick)

        @block.tensor
        def _(pe):
            def norm(n, c, what):
                part, step = what.split("_")
                w, j = CHUNKS[c][1], JOBS.index((n, c, part))
                if step == "stat":
                    pe.wait_ge(sem["ps"], j + 1)
                    wait(pe, "st", j)
                    for q in range(-(-w // P)):
                        v = min(P, w - q * P)
                        ins = pe.matmul(ps[0:v, 6, q:q + 1], PSa[:, q * P:q * P + v], ones[:, 0:1], start=True, stop=True)
                    ins.then_inc(sem["sta"], 1)
                else:
                    pe.wait_ge(sem["dg"], j + 1)
                    if j:
                        pn, pc, pp = JOBS[j - 1]
                        pe.wait_ge(sem["xs" if pp == "post" else "hs"], nth_of(pn, pc, pp) + 1)
                    for q in range(-(-w // P)):
                        v = min(P, w - q * P)
                        ins = pe.matmul(ps[:, 7, q * P:q * P + v], ones[0:v, :], DG[0:v, q * P:q * P + v], start=True, stop=True)
                    ins.then_inc(sem["rb"], 1)

            def norm_at(n, tick):
                for c, what in norm_pieces("pe", n, tick):
                    norm(n, c, what)

            def product(bank, w, c, slot, k, m, src, tiles, lo):
                t, p = m // 3, m % 3
                wt = (WH, WH, WL)[p][slot][:, (k + t) * P:(k + t + 1) * P]
                xt = ct((src, lo[0], src)[p], c, t + (0, lo[1], 0)[p])
                return pe.matmul(bank[:, 0:w], wt, xt, start=m == 0, stop=m == 3 * tiles - 1, skip_group_check=False)

            def step(bank, c, slot):
                for m in range(N_MM):
                    ins = product(bank, CHUNKS[c][1], c, slot, 0, m, XH, KT_D, (XL, 0))
                ins.then_inc(sem["D"], 1)

            def weights(sec, i, u):
                per = {"ATT": 3, "FF": 8}.get(sec.kind, 0)
                pe.wait_ge(sem["wlo"], sec.pick(i, sec.unit + u + 1, per))

            def h_ready(n, c):
                pe.wait_ge(sem["hlD"], nth_of(n, c, "pre") + 1)
                pe.wait_ge(sem["hlP"], nth_of(n, c, "pre") + 1)

            for name in ("S", "xpe"):
                pe.nop().then_inc(sem[name], 1)
            pe.wait_ge(sem["ones"], 2)
            for c in range(3):
                norm(0, c, "pre_stat")
                norm(0, c, "pre_bc")
            for sec in SECTIONS:
                if sec.kind == "T0":
                    for s in range(3 * sec.units):
                        c, u = (s // 3, s % 3) if s < 9 else (s - 9, 3)
                        if s >= 2:
                            pe.wait_ge(sem["evA"], sec.at(None, "evA", s - 1))
                        else:
                            wait(pe, "evD", sec.at(None, "evD", s - 5))
                        if c == 0:
                            weights(sec, None, u)
                        if u == 0:
                            h_ready(2 * sec.layer, c)
                        step(ps[:, s % 2, :], c, u)
                        if sec.layer == 1:
                            norm_at(2, NORM_ON + s)
                elif sec.kind == "ATT":
                    kind = sec.att
                    if sec.g0 % GROUPS == 0:
                        pe.wait_ge(sem["pad"], 2 * (sec.layer + 1))
                        pe.wait_ge(sem["hs"], nth_of(2 * sec.layer, 2, "pre") + 1)
                    with runs(pe, sec) as i:
                        def scores(s, m):
                            q0, k0, n, _ = block_of(kind, ORDER[s])
                            wait(pe, "ttr", sec.at(i, "ttr", 2 * (s - 1) + m + 1 if s else 0))
                            if s == 0:
                                pe.wait_ge(sem["qklo"], sec.at(i, "qklo", 2))
                            rows = slice(64 * m, 64 * m + 64)
                            for b, o in enumerate(range(0, n, 512)):
                                w = min(512, n - o)
                                out = ps[:, 2 + 2 * m + b, :]
                                q, k = slice(q0, q0 + P), slice(k0 + o, k0 + o + w)
                                pe.matmul(out[:, 0:w], Qh[rows, q], Kh[rows, k], start=True, stop=False)
                                if kind == "B" and o + w == n:
                                    v = N_SAMPLE if ORDER[s] == SAMPLE else P
                                    pe.matmul(out[:, w - v:w], identb[:, :], trib[:, 0:v], start=False, stop=False)
                                pe.matmul(out[:, 0:w], Qh[rows, q], Kl[rows, k], start=False, stop=False)
                                ins = pe.matmul(out[:, 0:w], Ql[rows, q], Kh[rows, k], start=False, stop=True)
                            ins.then_inc(sem["S"], 1)

                        def use_bank(use, s):
                            if use.prev is None:
                                wait(pe, "xA", sec.at(i, "xA"))
                                wait(pe, "xD", sec.at(i, "xD"))
                            else:
                                name = "x" + use.prev.engine
                                pe.wait_ge(sem[name], sec.at(i, name, use.prev.nth))
                            bank = ps[:, 6 + use.bank, :]
                            if use.what == "V":
                                pe.wait_ge(sem["evA"], sec.at(i, "evA"))
                                for k, t in enumerate(use.tiles):
                                    t0, v = (t * P, P) if t < 8 else (N_PROMPT, N_SAMPLE)
                                    ins = pe.transpose(bank[0:v, k * P:(k + 1) * P], VT[:, t0:t0 + v], ident[:, :])
                            elif use.what == "T":
                                k, st = s - 1, (s - 1) % 2
                                if kind == "A":
                                    pe.wait_ge(sem["comb"], sec.at(i, "comb", k + 1))
                                else:
                                    pe.wait_ge(sem["ex"], sec.at(i, "ex", 2 * k + use.m + 1))
                                for n, (o, v, _) in enumerate(use.tiles):
                                    ins = pe.transpose(bank[0:v, n * P:(n + 1) * P], PR[:, st, use.m, o:o + v], ident[:, :])
                            elif use.what == "OT":
                                k = s - 2
                                if kind == "A":
                                    pe.wait_ge(sem["on2"], sec.at(i, "on2", k + 1))
                                else:
                                    pv = [v for v in USES[kind][1] if v.what == "PV" and v.block == use.block][0]
                                    pe.wait_ge(sem["xD"], sec.at(i, "xD", pv.nth))
                                ins = pe.transpose(bank[:, 0:P], ON[:, :], ident[:, :])
                            else:
                                before = [v for v in USES[kind][1][:use.n] if v.what in ("V", "T")]
                                for e in "AD":
                                    nth = max(v.nth for v in before if v.engine == e)
                                    pe.wait_ge(sem["x" + e], sec.at(i, "x" + e, nth))
                                if use.block == SAMPLE:
                                    pe.wait_ge(sem["vc"], sec.at(i, "vc", 16))
                                for m in range(1 if kind == "A" else 2):
                                    f = slice(0, P) if kind == "A" else slice(64 * m, 64 * m + 64)
                                    for n, (o, v, t) in enumerate(use.tiles):
                                        ins = pe.matmul(bank[:, f], PT[0:v, m, o // P, :], V[0:v, t, f],
                                                        start=n == 0, stop=n == len(use.tiles) - 1)
                            ins.then_inc(sem["xpe"], 1)

                        for s in range(11):
                            uses = USES[kind][0][s]
                            last = 23 if s and S_AT[min(s, 8)] < 12 else 10
                            early = [use for use in uses if use.what in ("T", "V")]
                            at = {use: 1 + last * k // len(early) for k, use in enumerate(early)}
                            at.update({use: N_MM for use in uses if use not in early})
                            if s < 9 and sec.proj:
                                c, u = s // 3, s % 3
                                if s == 0:
                                    pe.wait_ge(sem["evA"], sec.at(i, "evA"))
                                elif s >= 2:
                                    pe.wait_ge(sem["evA"], sec.at(i, "evA", s - 1))
                                if c == 0:
                                    weights(sec, i, u)
                            for m in range(N_MM + 1):
                                if s < 9 and S_AT[s] == m:
                                    scores(s, 0)
                                    scores(s, 1)
                                for use in uses:
                                    if at[use] == m:
                                        use_bank(use, s)
                                if s < 9 and sec.proj and m < N_MM:
                                    ins = product(ps[:, s % 2, :], CHUNKS[c][1], c, u, 0, m, XH, KT_D, (XL, 0))
                                    if m == N_MM - 1:
                                        ins.then_inc(sem["D"], 1)
                elif sec.kind == "OUT":
                    pe.wait_ge(sem["evA"], sec.at(None, "evA"))
                    for name in ("ttr", "xA", "xD", "olo"):
                        pe.wait_ge(sem[name], sec.at(None, name))
                    for t in range(24):
                        q, c, u = t // 12, t % 12 // 4, t % 4
                        if t >= 6:
                            pe.wait_ge(sem["evA"], sec.at(None, "evA", t - 5))
                        if c == 0:
                            weights(sec, None, 4 * q + u)
                        step(ps[:, t % 6, :], c, u)
                        norm_at(1 + 2 * sec.layer, t - 15)
                else:
                    with runs(pe, sec) as i:
                        for t in range(12):
                            c, u = t // 4, t % 4
                            if t >= 6 or sec.f == 0:
                                pe.wait_ge(sem["evA"], sec.at(i, "evA", t - 5))
                            else:
                                pe.wait_ge(sem["evD"], sec.at(i, "evD", t - 5))
                            if c == 0:
                                weights(sec, i, u)
                            if sec.f == 0 and u == 0:
                                h_ready(1 + 2 * sec.layer, c)
                            step(ps[:, t % 6, :], c, u)
                            if sec.f == 0:
                                norm_at(1 + 2 * sec.layer, NORM_ON + t)
                        for t in range(12):
                            c, u = t // 4, t % 4
                            if c == 0:
                                weights(sec, i, 4 + u)
                            if u == 0:
                                pe.wait_ge(sem["uu"], sec.at(i, "uu", 4 * (c + 1)))
                            for v in (2 * t, 2 * t + 1):
                                if v < 6:
                                    pe.wait_ge(sem["evA"], sec.at(i, "evA", 7 + v))
                                else:
                                    pe.wait_ge(sem["evD"], sec.at(i, "evD", v - 5))
                                for m in range(N_MM // 2):
                                    ins = product(ps[:, v % 6, :], CHUNKS[c][1], c, u, 4 * (v % 2), m, U, 4, (U, 4))
                                ins.then_inc(sem["D"], 1)
                            if sec.last:
                                norm_at(2 + 2 * sec.layer, t - 3)
                    if sec.last and sec.layer == 1:
                        for tick in range(NORM_ON, LAST_TICK + 1):
                            norm_at(4, tick)


def kernel(**inputs):
    import numpy as np
    import ml_dtypes
    import concourse.bacc as bacc
    from concourse.bass_utils import run_bass_kernel_spmd as run

    a = {name: np.asarray(v) for name, v in inputs.items()}

    def feature_major(x):
        t = x.T.reshape(KT_D, P, TOK).transpose(1, 0, 2)
        return np.concatenate([t[:, :, o:o + w].reshape(P, -1) for o, w in CHUNKS], axis=1)

    def unit(w):
        return w.reshape(KT_D, P, P).transpose(1, 0, 2).reshape(1, P, KT_D * P)

    def columns(w, c0):
        return unit(w[:, c0:c0 + P])

    def mlp_units(up, down):
        out = []
        for f in range(FF_GROUPS):
            out += [columns(up, (4 * f + u) * P) for u in range(4)]
            d = down[4 * P * f:4 * P * (f + 1)].reshape(4, P, 4, 2, P)
            out += [d[:, :, u].transpose(1, 2, 0, 3).reshape(1, P, -1) for u in range(4)]
        return out

    we, wo = a["w_in_even"][0], a["w_in_odd"][0]
    qk, v0 = 512, 1024
    cols = [(h * P, qk + h * P, v0 + h * P) for h in range(4)] + [(1536 + j * P, 2048 + j * P, 2560 + j * P) for j in range(4)]
    units = [columns(we, c) for c in cols[0]]
    gate = np.zeros((D_MODEL, P), np.float32)
    gate[:, 0:8] = we[:, 3072:3080]
    units.append(unit(gate))
    units += [columns(we, c) for group in cols[1:] for c in group]
    units += [columns(a["w_out_even"][0], o * P) for o in range(8)] + mlp_units(a["w_ffn_up"][0], a["w_ffn_down"][0])
    units += [columns(wo, s * D_MODEL + j * P) for j in range(8) for s in range(3)]
    units += [columns(a["w_out_odd"][0], o * P) for o in range(8)] + mlp_units(a["w_ffn_up"][1], a["w_ffn_down"][1])
    assert len(units) == UNITS

    gains = np.concatenate([a["g_" + which][layer].reshape(KT_D, P).T for which, layer in GAINS], axis=1)

    def k_tiles(cache, n):
        return cache.reshape(N_CACHE, n, P).transpose(1, 2, 0)

    def v_tiles(cache, n):
        return cache.reshape(2, P, n, P).transpose(2, 1, 0, 3)

    kcache = np.concatenate([k_tiles(a["cache_a_k"][0, 0], 4), k_tiles(a["cache_b_k"][0, 0], 4), k_tiles(a["cache_c_k"][0, 0], 8)])
    vcache = np.concatenate([v_tiles(a["cache_a_v"][0, 0], 4), v_tiles(a["cache_b_v"][0, 0], 4), v_tiles(a["cache_c_v"][0, 0], 8)])
    q, k = np.arange(P)[:, None], np.arange(1024)[None, :] - (1024 - P)
    dist = np.where(k // 64 <= q // 64, -np.abs(q - k).astype(np.float32), 0)
    alibi = np.stack([np.where(k // 64 <= q // 64, dist * 2.0 ** (-8.0 * (h + 1) / 4), NEG) for h in range(4)]).astype(np.float32)
    causal = np.where(np.arange(P)[None, :] <= np.arange(P)[:, None], 0, NEG).astype(ml_dtypes.bfloat16)
    x = np.concatenate([a["x_prompt"][0], a["x_sample"][0]])
    arrays = dict(
        x_in=feature_major(x), w_in=np.concatenate(units), gains_in=gains, subg_in=a["subln_g"][0].reshape(P, 1),
        bf_in=a["b_forget"][0].reshape(8, 1), lam_in=np.concatenate([a[n] for n in ("lam_q1", "lam_k1", "lam_q2", "lam_k2")]),
        kcache=kcache, vcache=vcache, logf_cache=a["cache_b_logf"][0, 0].T, alibi=alibi, rel_bias=a["rel_bias"][0],
        ident_in=np.eye(P, dtype=np.float32), identb_in=np.eye(P).astype(ml_dtypes.bfloat16), tri_in=causal)
    outputs = dict(y_out=(P, 8 * TOK), k_out=(16, P, KCOLS), v_out=(16, P, TOK), logf_out=(8, TOK), vband_out=(8, P, 2, P))

    nc = bacc.Bacc("TRN2", target_bir_lowering=False, num_devices=1)
    args = {}
    for name, v in arrays.items():
        arrays[name] = v = np.ascontiguousarray(v)
        args[name] = nc.dram_tensor(name, v.shape, mybir.dt.from_np(v.dtype), kind="ExternalInput").ap()
    for name, shape in outputs.items():
        args[name] = nc.dram_tensor(name, shape, mybir.dt.float32, kind="ExternalOutput").ap()
    build_program(nc, **args)
    r = run(nc, [arrays], core_ids=[0]).results[0]

    y = r["y_out"]
    y = np.concatenate([y[:, 8 * o:8 * (o + w)].reshape(P, KT_D, w) for o, w in CHUNKS], axis=2)
    y = y.transpose(2, 1, 0).reshape(TOK, D_MODEL)

    def rows(t, heads):
        n = t.shape[2]
        return t.transpose(2, 0, 1).reshape(1, 1, n, heads, -1)

    kk, vv = r["k_out"], r["v_out"]
    kp, ks, vp, vs = kk[:, :, 0:N_PROMPT], kk[:, :, N_PROMPT + N_CACHE:], vv[:, :, 0:N_PROMPT], vv[:, :, N_PROMPT:]
    lf = r["logf_out"]
    v_past = r["vband_out"].transpose(0, 3, 2, 1).reshape(8, P, N_CACHE)
    band_v = np.concatenate([v_past[:, :, N_SAMPLE:], vs[8:]], axis=2)
    return (y[None, 0:N_PROMPT], y[None, N_PROMPT:],
            rows(kp[0:4], 4), rows(vp[0:4], 4), rows(kp[4:8], 8), rows(vp[4:8], 8), lf[:, 0:N_PROMPT].T[None, None],
            rows(kp[8:, :, 512:], 16), rows(vp[8:, :, 512:], 16),
            rows(ks[0:4], 4), rows(vs[0:4], 4), rows(ks[4:8], 8), rows(vs[4:8], 8), lf[:, N_PROMPT:].T[None, None],
            rows(kk[8:, :, N_PROMPT + N_SAMPLE:], 16), rows(band_v, 16))
```

```python
import concourse.bass as bass
from concourse import mybir
from contextlib import ExitStack, contextmanager

P = 128
D_MODEL, D_FF = 1024, 4096
KT_D = D_MODEL // P
N_PROMPT, N_SAMPLE, N_CACHE = 1024, 64, 256
TOK = N_PROMPT + N_SAMPLE
CHUNKS = [(0, 384), (384, 384), (768, 320)]
GROUPS = 8
FF_GROUPS = 8
KCOLS = N_PROMPT + N_CACHE + N_SAMPLE
QCOLS = TOK + 64
C_BAND = 640
SAMPLE = 8
ORDER = [7, 6, 5, 4, 3, 2, 1, SAMPLE, 0]
S_AT = {k: [24, 8, 4, 0, 0, 0, 0, 0, 0] for k in "ABC"}
S_AT["alone"] = [0] + [12] * 8
T_AT = {k: [(12, 22)] * 8 + [(2, 6), (9, 13), (14, 24)] for k in "ABC"}
T_AT["alone"] = [(1, 11)] * 11
SLOT_PRODUCTS = [(0, 3 * KT_D)] * 8 + [(0, 6), (6, 14), (14, 3 * KT_D)]
NEG = -1e30
EPS = 1e-6
LAM_INIT = 0.2
N_MM = 3 * KT_D


def block_of(kind, b):
    if b == SAMPLE:
        n = N_CACHE + N_SAMPLE
        return N_PROMPT, N_PROMPT, n, {"A": 1024 - 3 * P, "B": N_PROMPT, "C": C_BAND - 3 * P}[kind]
    n = P * (b + 1) if kind != "C" else min(C_BAND, P * (b + 1))
    k0 = P * (b + 1) - n
    return P * b, k0, n, {"A": 1024 - n, "B": k0, "C": C_BAND - n}[kind]


def banks_of(n):
    return -(-n // 512)


def key_tiles(kind, b):
    _, k0, n, _ = block_of(kind, b)
    first = SAMPLE if b == SAMPLE else k0 // P
    return [(o, min(P, n - o), first + o // P) for o in range(0, n, P)]


class Use:

    def __init__(self, what, block, m, tiles, engine):
        self.what, self.block, self.m, self.tiles, self.engine = what, block, m, tiles, engine


def bank_uses(kind):
    slots = [[] for _ in range(11)]
    for n, t in enumerate(([0, 1, 2], [3, 4, 5, 6], [7, SAMPLE + 2])):
        slots[0].append(Use("V", None, 0, t, "AD"[n % 2]))
    for s in range(1, 11):
        ot = [Use("OT", ORDER[s - 2], 0, [], "A")] if s >= 2 else []
        if s == 10:
            slots[s] += ot
        else:
            b = ORDER[s - 1]
            tiles = key_tiles(kind, b)
            n = 0
            for m in range(1 if kind == "A" else 2):
                for o in range(0, len(tiles), 4):
                    slots[s].append(Use("T", b, m, tiles[o:o + 4], "AD"[n % 2]))
                    n += 1
            slots[s] += ot + [Use("PV", b, 0, tiles, "D")]
    flat = [u for slot in slots for u in slot]
    count = {"A": 0, "D": 0}
    for n, u in enumerate(flat):
        u.n = n
        count[u.engine] += 1
        u.nth = count[u.engine]
        u.bank = n % 2
        u.prev = flat[n - 2] if n >= 2 else None
    return slots, flat, count


USES = {k: bank_uses(k) for k in "ABC"}


class Section:

    def __init__(self, kind, layer, reps, per, units=0, att="", g0=0, proj=False, f=0, last=False, nxt=0):
        self.kind, self.layer, self.reps, self.per = kind, layer, reps, per
        self.units = units
        self.att, self.g0, self.proj = att, g0, proj
        self.f, self.last, self.nxt = f, last, nxt
        self.base, self.unit, self.loaded = {}, 0, 0

    def at(self, i, name, k=0):
        v = self.base.get(name, 0) + k
        return v if self.reps == 1 else i * self.per.get(name, 0) + v

    def end(self, name):
        return self.base.get(name, 0) + self.per.get(name, 0) * self.reps

    def pick(self, i, first, per):
        return first if self.reps == 1 else i * per + first


STAGE = [0, 1, 2, 0]


def stage_loads(units):
    return {f"ld{s}": 16 * sum(STAGE[u] == s for u in units) for s in range(3)}


def add(*counts):
    out = {}
    for c in counts:
        for name, v in c.items():
            out[name] = out.get(name, 0) + v
    return out


FROM_ONE = ("S", "ttr", "xpe", "xA", "xD")


def make_sections():
    out = []
    triple, quad = stage_loads(range(3)), stage_loads(range(4))

    def attention(layer, kind, g0, reps, proj):
        _, flat, count = USES[kind]
        per = dict(qkhi=2, qklo=2, S=18, ttr=18, nm=18, ex=18, ri=9, xpe=len(flat), xA=count["A"], xD=count["D"],
                   bias=16 if kind == "A" else 32, vc=16, kst=16, vst=16)
        if kind == "A":
            per.update(cs=9, comb=9, ms=9, rs=9, on2=9)
        if kind == "C":
            per.update(cm=1)
        if proj:
            per = add(per, dict(D=9, evA=9, whi=3, wlo=3, kc=16, ost=16), triple)
        else:
            per = add(per, dict(whi=1, wlo=1, ld0=16, os0=64, os1=48, ohi=8, olo=8))
        out.append(Section("ATT", layer, reps, per, units=3 * proj, att=kind, g0=g0, proj=proj))

    for layer in (0, 1):
        n = 4 if layer == 0 else 3
        out.append(Section("T0", layer, 1, add(dict(D=3 * n, evA=3 * n, whi=3, wlo=3, kc=16), triple), units=n))
        if layer == 0:
            attention(0, "A", 0, 4, True)
            attention(0, "B", 4, 3, True)
            attention(0, "B", 7, 1, False)
        else:
            attention(1, "C", 8, 7, True)
            attention(1, "C", 15, 1, False)
        out.append(Section("OUT", layer, 1, add(dict(D=24, evA=24, whi=8, wlo=8), quad, quad), units=8))
        for f, reps in ((0, 1), (1, FF_GROUPS - 2), (FF_GROUPS - 1, 1)):
            last = f == FF_GROUPS - 1
            nxt = 4 if not last else 3 if layer == 0 else 0
            per = add(dict(D=36, evA=12, evD=24, uhi=12, um=12, uu=12, whi=4 + nxt, wlo=4 + nxt), quad, stage_loads(range(nxt)))
            out.append(Section("FF", layer, reps, per, units=8, f=f, last=last, nxt=nxt))
    base, unit, loaded = add(dict(whi=4, wlo=4), quad, {name: 1 for name in FROM_ONE}), 0, 4
    for s in out:
        s.base, s.unit, s.loaded = dict(base), unit, loaded
        unit += s.reps * s.units
        loaded += s.reps * s.per["wlo"]
        base = add(base, {name: v * s.reps for name, v in s.per.items()})
    assert base["wlo"] == unit == loaded
    return out, base, unit


SECTIONS, TOTALS, UNITS = make_sections()


def section(kind, layer, last=False):
    return next(s for s in SECTIONS if s.kind == kind and s.layer == layer and (not last or s.last))


NORMS = {0: dict(pre=("pre_mix", 0)), 1: dict(post=("post_mix", 0), pre=("pre_ffn", 0)),
         2: dict(post=("post_ffn", 0), pre=("pre_mix", 1)), 3: dict(post=("post_mix", 1), pre=("pre_ffn", 1)),
         4: dict(post=("post_ffn", 1))}
JOBS = [(n, c, part) for n in range(5)
        for c, part in ((0, "post"), (0, "pre"), (1, "post"), (2, "post"), (1, "pre"), (2, "pre")) if part in NORMS[n]]
GAINS = [(which, layer) for which in ("pre_mix", "post_mix", "pre_ffn", "post_ffn") for layer in (0, 1)]


def nth_of(n, c, part):
    return [j for j in JOBS if j[2] == part].index((n, c, part))


PLAN = {
    "act": [("pre_sq", 2, 7, 10), ("pre_hi", 5, 10, 13)],
    "dve": [("post_diag", 0, 4, 8), ("post_x", 1, 6, 9), ("pre_red", 3, 8, 11), ("pre_diag", 4, 9, 12),
            ("pre_h", 5, 10, 13), ("pre_lo", 6, 11, 14)],
    "pe": [("post_stat", 0.5, 4.5, 8.5), ("post_bc", 1.5, 5.5, 9.5), ("pre_stat", 4.5, 9.5, 12.5), ("pre_bc", 5.5, 10.5, 13.5)],
    "pool": [("post_load", 0, 4, 8), ("post_pow", 0, 4, 8), ("post_x", 1, 6, 9), ("pre_pow", 4, 9, 12), ("pre_lo", 6, 11, 14)],
}
LAST_TICK = 14


def norm_pieces(engine, n, tick):
    out = [(c, what) for what, *at in PLAN[engine] for c in range(3) if at[c] == tick and what.split("_")[0] in NORMS[n]]
    return sorted(out, key=lambda p: JOBS.index((n, p[0], p[1].split("_")[0])))


SQUARES = 3 * KT_D


def square_of(n, t):
    if n % 2:
        return t % 12 // 4, t % 4 == 0 and t < 12
    return t // KT_D, t % KT_D == 0


NORM_ON = 9


def build_program(nc, x_in, w_in, gains_in, subg_in, bf_in, lam_in, kcache, vcache, logf_cache, alibi, rel_bias,
                  ident_in, identb_in, tri_in, y_out, k_out, v_out, logf_out, vband_out):
    f32, f32r, bf16 = mybir.dt.float32, mybir.dt.float32r, mybir.dt.bfloat16
    ALU, ACT, AX = mybir.AluOpType, mybir.ActivationFunctionType, mybir.AxisListType
    ctx = ExitStack()
    with ctx:
        spot = [-(-nc.sbuf_base // 32) * 32]

        def place(name, offset, shape, dt=f32, size=4):
            for n in shape[1:]:
                size *= n
            assert offset + size <= nc.sbuf_usable_end, (name, offset, size)
            return nc.alloc_sbuf_tensor_at(name, shape, dt, offset=offset), offset + -(-size // 32) * 32

        def own(name, shape, dt=f32, size=4):
            t, spot[0] = place(name, spot[0], shape, dt, size)
            return t

        XH, XL = own("XH", [P, 8 * TOK], f32r), own("XL", [P, 8 * TOK], f32r)
        WH = [own(f"WH{s}", [P, 8 * P], f32r) for s in range(4)]
        WL = [own(f"WL{s}", [P, 8 * P], f32r) for s in range(4)]
        WS = [own(f"WS{s}", [P, 8 * P]) for s in range(3)]
        ident, ones = own("ident", [P, P]), own("ones", [P, P])
        identb, trib = own("identb", [P, P], bf16, 2), own("trib", [P, P], bf16, 2)
        G = own("G", [P, 8 * KT_D])
        subg, bF, nlam = own("subg", [P, 1]), own("bF", [8, 1]), own("nlam", [P, 1])
        halfpow = own("halfpow", [P, 3])
        ST, RS = own("ST", [P, 3]), own("RS", [P, 3])
        M, NM, L, RI = (own(n, [P, 4]) for n in ("M", "NM", "L", "RI"))
        CS, MS, RSO = (own(n, [P, 2]) for n in ("CS", "MS", "RSO"))
        hold = own("hold", [P, 1])

        r, xb = spot[0], 8 * TOK * 4
        XRES, _ = place("XRES", r, [P, 8 * TOK])
        U, _ = place("U", r, [P, 8 * TOK], f32r)
        ACC, z = place("ACC", r + xb, [P, 8 * TOK])
        QT, z1 = place("QT", z, [P, TOK])
        KT, z1 = place("KT", z1, [P, KCOLS])
        VT, z1 = place("VT", z1, [P, TOK])
        TU, z2 = place("TU", z, [P, 2, 384])
        TS, _ = place("TS", z2, [P, 2, 384])
        SQ, z1 = place("SQ", z1, [P, 2, 384])
        PSO, z1 = place("PSO", z1, [P, TOK])
        PSX, z1 = place("PSX", z1, [P, 384])
        DG, z1 = place("DG", z1, [P, 2, 384])
        Qh, a = place("Qh", r, [P, QCOLS], f32r)
        Ql, a = place("Ql", a, [P, QCOLS], f32r)
        Kh, a = place("Kh", a, [P, KCOLS], f32r)
        Kl, a = place("Kl", a, [P, KCOLS], f32r)
        V, a = place("V", a, [P, 11, P])
        BIAS, a = place("BIAS", a, [P, 2, KCOLS])
        f0 = a
        PR, a = place("PR", a, [P, 2, 2, N_PROMPT])
        PT, a = place("PT", a, [P, 2, 8, P])
        OT, a = place("OT", a, [P, TOK])
        ON, a = place("ON", a, [P, P])
        assert a <= z
        ZF, f1 = place("ZF", f0, [8, KCOLS])
        FA, f1 = place("FA", f1, [8, KCOLS])
        LF, f1 = place("LF", f1, [8, KCOLS])
        NC, f1 = place("NC", f1, [8, KCOLS])
        ZZ, f1 = place("ZZ", f1, [8, KCOLS])
        LQ, f1 = place("LQ", f1, [P, 4, 64])
        LP, f1 = place("LP", f1, [P, 2])
        assert f1 <= z
        RB0, z3 = place("RB0", z, [16, 513])
        RB1, z3 = place("RB1", z3, [16, 768])

        x_scr = [nc.dram_tensor(f"x_scr{n}", (P, 8 * TOK), f32).ap() for n in range(3)]
        o_scr = nc.dram_tensor("o_scr", (GROUPS, P, TOK), f32).ap()
        nc_scr = nc.dram_tensor("nc_scr", (8, KCOLS), f32).ap()
        rel_t = nc.dram_tensor("rel_scr", (16, 768), f32)
        toep_scr = nc.dram_tensor("toep_scr", (16, P, C_BAND), f32).ap()

        ps = ctx.enter_context(nc.psum_tensor("ps", [P, 8, 512], f32))

        def semaphore(name):
            return ctx.enter_context(nc.semaphore("s_" + name))

        names = ("D evA evD "
                 "ld0 ld1 ld2 whi wlo "
                 "qkhi qklo kc vc kst vst bias cm "
                 "S ttr nm ex ri cs comb "
                 "xpe xA xD "
                 "ms rs on2 "
                 "ost os0 os1 ohi olo "
                 "uhi um uu").split()
        sem = {n: semaphore(n) for n in names}
        sem.update({n: semaphore(n) for n in (
            "xl0 xl1 xl2 xst0 xst1 xst2 "
            "sqo sum sqx ps sta st pw dg rb xs xuD xuP hs hh hlD hlP").split()})
        sem.update({n: semaphore(n) for n in "const pad ones fabs fexp flog fl flogf fscan fst lamdot lamexp lam rbias rel rels toep vb".split()})
        block = ctx.enter_context(nc.Block())

        def wait(eng, name, value):
            if not isinstance(value, int) or value > 0:
                eng.wait_ge(sem[name], value)

        @contextmanager
        def runs(eng, sec):
            if sec.reps == 1:
                yield None
            else:
                with eng.Fori(0, sec.reps, 1) as i:
                    yield i

        def ct(buf, c, k, n=1):
            o, w = CHUNKS[c]
            return buf[:, 8 * o + k * w:8 * o + (k + n) * w]

        def gain(which, k):
            j = KT_D * GAINS.index(which) + k
            return G[:, j:j + 1]

        def norms_over(eng, first_attention):
            n = 0 if first_attention.layer == 0 else 2
            wait(eng, "hh", 2 * nth_of(n, 2, "pre") + 2)
            for name in ("hlD", "hlP"):
                wait(eng, name, nth_of(n, 2, "pre") + 1)
            for c in range(3):
                wait(eng, f"xst{c}", 16 * n)
            wait(eng, "fst", 48)

        def transposed(use, bank):
            rows = [P if use.what == "V" and t != SAMPLE + 2 else N_SAMPLE if use.what == "V" else t[1] for t in use.tiles]
            first = use.tiles[0] if use.what == "V" else use.tiles[0][0] // P
            buf = V[:, :, :] if use.what == "V" else PT[:, use.m, :, :]
            full = sum(n == P for n in rows)
            out = []
            if full:
                out.append((buf[:, first:first + full, :].rearrange("p t q -> p (t q)"), bank[:, 0:full * P]))
            if full < len(rows):
                last = use.tiles[-1] if use.what == "V" else first + full
                out.append((buf[0:N_SAMPLE, last, :], bank[0:N_SAMPLE, full * P:(full + 1) * P]))
            return out

        @block.sync
        def _(sp):
            def load_unit(sec, i, k, u, prev):
                n = sec.pick(i, sec.loaded + k, sec.per["wlo"])
                wait(sp, "wlo", sec.pick(i, sec.loaded + k - prev + 1, sec.per["wlo"]))
                sp.dma_start(WS[STAGE[u]][:, :], w_in[n, :, :]).then_inc(sem[f"ld{STAGE[u]}"], 16)

            def load_quad(sec, i, k, units=4):
                for u in range(units):
                    load_unit(sec, i, k + u, u, (1, 4, 4, 3)[u])

            for dst, src in ((ident, ident_in), (identb, identb_in), (trib, tri_in), (G, gains_in), (subg, subg_in), (bF, bf_in)):
                sp.dma_start(dst[:, :], src).then_inc(sem["const"], 16)
            for u in range(3):
                sp.dma_start(WS[u][:, :], w_in[u, :, :]).then_inc(sem[f"ld{u}"], 16)
            sp.dma_start(RB0[:, :], rel_bias).then_inc(sem["rbias"], 16)
            sp.wait_ge(sem["wlo"], 1)
            sp.dma_start(WS[0][:, :], w_in[3, :, :]).then_inc(sem["ld0"], 16)
            sp.dma_start(vband_out, vcache[8:16, :, :, :]).then_inc(sem["vb"], 16)
            sp.wait_ge(sem["rel"], 3)
            sp.dma_start(rel_t.ap(), RB1[:, :]).then_inc(sem["rels"], 16)
            sp.wait_ge(sem["rels"], 16)
            sp.dma_start(toep_scr, bass.AP(rel_t, P - 1, [[768, 16], [-1, P], [1, C_BAND]])).then_inc(sem["toep"], 16)
            for sec in SECTIONS:
                if sec.kind == "T0":
                    wait(sp, "uu", sec.at(None, "uu"))
                    sp.dma_start(KT[:, N_PROMPT:N_PROMPT + N_CACHE], kcache[GROUPS * sec.layer, :, :]).then_inc(sem["kc"], 16)
                    for u in range(3):
                        load_unit(sec, None, u, u, (1, 4, 4)[u] if sec.layer == 0 else 3)
                    if sec.layer == 0:
                        sp.wait_ge(sem["D"], 10)
                        sp.dma_start(LF[:, N_PROMPT:N_PROMPT + N_CACHE], logf_cache).then_inc(sem["fl"], 16)
                        for k in range(4):
                            sp.dma_start(LQ[:, k, :], lam_in[k:k + 1, :].to_broadcast([P, 64])).then_inc(sem["fl"], 16)
                        sp.wait_ge(sem["flogf"], 2)
                        sp.dma_start(logf_out[:, 0:N_PROMPT], LF[:, 0:N_PROMPT]).then_inc(sem["fst"], 16)
                        sp.dma_start(logf_out[:, N_PROMPT:TOK], LF[:, N_PROMPT + N_CACHE:]).then_inc(sem["fst"], 16)
                        sp.wait_ge(sem["fscan"], 2)
                        sp.dma_start(nc_scr, NC[:, :]).then_inc(sem["fst"], 16)
                elif sec.kind == "ATT":
                    if sec.g0 % GROUPS == 0:
                        norms_over(sp, sec)
                        sp.wait_ge(sem["toep"], 16)
                    with runs(sp, sec) as i:
                        g = sec.pick(i, sec.g0, 1)
                        wait(sp, "ttr", sec.at(i, "ttr"))
                        if sec.att == "A":
                            sp.dma_start(BIAS[:, 0, 0:1024], alibi[g, :, :]).then_inc(sem["bias"], 16)
                        for m in range(2):
                            if sec.att == "B":
                                row = bass.AP(nc_scr.tensor, sec.pick(i, (2 * (sec.g0 - 4) + m) * KCOLS, 2 * KCOLS), [[0, P], [1, KCOLS]])
                                sp.dma_start(BIAS[:, m, :], row).then_inc(sem["bias"], 16)
                            elif sec.att == "C":
                                sp.dma_start(BIAS[:, m, 0:C_BAND], toep_scr[sec.pick(i, 2 * (sec.g0 - 8) + m, 2), :, :])\
                                    .then_inc(sem["bias"], 16)
                        wait(sp, "xpe", sec.at(i, "xpe"))
                        sp.dma_start(V[:, 8:10, :], vcache[g, :, :, :]).then_inc(sem["vc"], 16)
                        wait(sp, "evA", sec.at(i, "evA"))
                        sp.wait_ge(sem["kc"], sec.at(i, "kc"))
                        sp.dma_start(k_out[g, :, :], KT[:, :]).then_inc(sem["kst"], 16)
                        sp.dma_start(v_out[g, :, :], VT[:, :]).then_inc(sem["vst"], 16)
                        if sec.proj:
                            for u in range(3):
                                load_unit(sec, i, u, u, 3)
                            sp.wait_ge(sem["qkhi"], sec.at(i, "qkhi", 2))
                            sp.wait_ge(sem["qklo"], sec.at(i, "qklo", 2))
                            sp.wait_ge(sem["kst"], sec.at(i, "kst", 16))
                            sp.dma_start(KT[:, N_PROMPT:N_PROMPT + N_CACHE], kcache[sec.pick(i, sec.g0 + 1, 1), :, :])\
                                .then_inc(sem["kc"], 16)
                            sp.wait_ge(sem["xA"], sec.at(i, "xA", sec.per["xA"]))
                            sp.dma_start(o_scr[sec.pick(i, sec.g0 % GROUPS, 1), :, :], OT[:, :]).then_inc(sem["ost"], 16)
                        else:
                            load_unit(sec, i, 0, 3, 3)
                            for o in range(7):
                                sp.wait_ge(sem["ost"], sec.at(i, "ost"))
                                if o == 0:
                                    sp.wait_ge(sem["qklo"], sec.at(i, "qklo", 1))
                                elif o == 1:
                                    sp.wait_ge(sem["vst"], sec.at(i, "vst", 16))
                                    sp.wait_ge(sem["xpe"], sec.at(i, "xpe", 3))
                                else:
                                    sp.wait_ge(sem["olo"], sec.at(i, "olo", o - 1))
                                sp.dma_start((QT, VT)[o % 2][:, :], o_scr[o, :, :]).then_inc(sem[f"os{o % 2}"], 16)
                elif sec.kind == "OUT":
                    load_quad(sec, None, 0)
                    load_quad(sec, None, 4)
                else:
                    with runs(sp, sec) as i:
                        load_quad(sec, i, 0)
                        load_quad(sec, i, 4, sec.nxt)
            for name in ("kst", "vst", "ost"):
                sp.wait_ge(sem[name], TOTALS[name])
            sp.wait_ge(sem["fst"], 48)
            sp.wait_ge(sem["toep"], 16)
            sp.wait_ge(sem["vb"], 16)
            for c in range(3):
                sp.wait_ge(sem[f"xst{c}"], 64)

        @block.gpsimd
        def _(pool):
            def lo_unit(sec, i, k, u):
                pool.wait_ge(sem["whi"], sec.pick(i, sec.loaded + k + 1, sec.per["wlo"]))
                pool.tensor_tensor(WL[u][:, :], WS[STAGE[u]][:, :], WH[u][:, :].bitcast(f32), ALU.subtract)\
                    .then_inc(sem["wlo"], 1)

            def norm(n, c, what):
                o, w = CHUNKS[c]
                cols = slice(8 * o, 8 * (o + w))
                if what == "post_load" and n in (2, 4):
                    pool.wait_ge(sem["D"], section("FF", n // 2 - 1, True).at(None, "D", 12 + 8 * (c + 1)))
                    pool.wait_ge(sem[f"xst{c}"], 16 * (n - 1))
                    pool.dma_start(ct(XRES, c, 0, 8), x_scr[n - 2][:, cols]).then_inc(sem[f"xl{c}"], 16)
                elif what in ("post_pow", "pre_pow"):
                    j = JOBS.index((n, c, what[:-4]))
                    pool.wait_ge(sem["st"], j + 1)
                    full = w // P
                    ins = pool.tensor_tensor(RS[:, 0:full], ST[:, 0:full], halfpow[:, 0:full], ALU.pow)
                    if w % P:
                        h = w % P
                        ins = pool.tensor_tensor(RS[0:h, full:full + 1], ST[0:h, full:full + 1], halfpow[0:h, 0:1], ALU.pow)
                    ins.then_inc(sem["pw"], 1)
                elif what == "post_x":
                    j = nth_of(n, c, "post")
                    pool.wait_ge(sem["xs"], 2 * j + 1)
                    pool.wait_ge(sem[f"xl{c}"], 16 * (n + 1))
                    pool.tensor_tensor(ct(XRES, c, 0, 4), ct(XRES, c, 0, 4), ct(ACC, c, 0, 4), ALU.add).then_inc(sem["xuP"], 1)
                    pool.wait_ge(sem["xuP"], j + 1)
                    pool.wait_ge(sem["xuD"], j + 1)
                    dst = y_out if n == 4 else x_scr[n - 1]
                    pool.dma_start(dst[:, cols], ct(XRES, c, 0, 8)).then_inc(sem[f"xst{c}"], 16)
                elif what == "pre_lo":
                    j = nth_of(n, c, "pre")
                    pool.wait_ge(sem["hh"], 2 * j + 1)
                    pool.tensor_tensor(ct(XL, c, 0, 4), ct(ACC, c, 0, 4), ct(XH, c, 0, 4).bitcast(f32), ALU.subtract)\
                        .then_inc(sem["hlP"], 1)

            def norm_at(n, tick):
                for c, what in norm_pieces("pool", n, tick):
                    norm(n, c, what)

            def sum_square(n, t):
                c, first = square_of(n, t)
                o, w = CHUNKS[c]
                pool.wait_ge(sem["sqo"], SQUARES * (n - 1) + t + 1)
                if first:
                    pool.tensor_copy(PSO[:, o:o + w], SQ[:, t % 2, 0:w]).then_inc(sem["sum"], 1)
                else:
                    pool.wait_ge(sem["sum"], SQUARES * (n - 1) + t)
                    pool.tensor_tensor(PSO[:, o:o + w], PSO[:, o:o + w], SQ[:, t % 2, 0:w], ALU.add).then_inc(sem["sum"], 1)

            first = Section("START", 0, 1, dict(wlo=4))
            for c, (o, w) in enumerate(CHUNKS):
                pool.dma_start(ct(XRES, c, 0, 8), x_in[:, 8 * o:8 * (o + w)]).then_inc(sem[f"xl{c}"], 16)
            pool.memset(ones[:, :], 1.0).then_inc(sem["ones"], 1)
            pool.memset(halfpow[:, :], -0.5).then_inc(sem["ones"], 1)
            pool.wait_ge(sem["ones"], 2)
            norm(0, 0, "pre_pow")
            lo_unit(first, None, 0, 0)
            norm(0, 0, "pre_lo")
            lo_unit(first, None, 1, 1)
            norm(0, 1, "pre_pow")
            lo_unit(first, None, 2, 2)
            norm(0, 1, "pre_lo")
            lo_unit(first, None, 3, 3)
            norm(0, 2, "pre_pow")
            norm(0, 2, "pre_lo")
            for sec in SECTIONS:
                if sec.kind == "T0":
                    for s in range(9):
                        if s >= 6:
                            lo_unit(sec, None, s - 6, s - 6)
                        if sec.layer == 1:
                            norm_at(2, NORM_ON + s)
                elif sec.kind == "ATT":
                    if sec.g0 % GROUPS == 0:
                        norms_over(pool, sec)
                        pool.memset(Qh[:, TOK:QCOLS].bitcast(f32), 0.0).then_inc(sem["pad"], 1)
                        pool.memset(Ql[:, TOK:QCOLS].bitcast(f32), 0.0).then_inc(sem["pad"], 1)
                    with runs(pool, sec) as i:
                        def rstd(k):
                            q = k % 2
                            pool.wait_ge(sem["ms"], sec.at(i, "ms", k + 1))
                            pool.tensor_tensor(RSO[:, q:q + 1], MS[:, q:q + 1], halfpow[:, 0:1], ALU.pow)\
                                .then_inc(sem["rs"], 1)

                        for s in range(9):
                            if sec.att == "A" and s >= 1:
                                rstd(s - 1)
                            if sec.att == "A" and s == 8:
                                rstd(8)
                            if sec.proj and s >= 6:
                                lo_unit(sec, i, s - 6, s - 6)
                        if not sec.proj:
                            lo_unit(sec, i, 0, 3)
                            for o in range(8):
                                pool.wait_ge(sem["ohi"], sec.at(i, "ohi", o + 1))
                                src = (QT, VT)[o % 2] if o < 7 else OT
                                for c, (t0, w) in enumerate(CHUNKS):
                                    ins = pool.tensor_tensor(ct(XL, c, o), src[:, t0:t0 + w], ct(XH, c, o).bitcast(f32), ALU.subtract)
                                ins.then_inc(sem["olo"], 1)
                elif sec.kind == "OUT":
                    n = 1 + 2 * sec.layer
                    pool.wait_ge(sem["D"], sec.at(None, "D", 1))
                    for c, (t0, w) in enumerate(CHUNKS):
                        if n == 3:
                            pool.wait_ge(sem[f"xst{c}"], 32)
                        src = x_in if n == 1 else x_scr[1]
                        pool.dma_start(ct(XRES, c, 0, 8), src[:, 8 * t0:8 * (t0 + w)]).then_inc(sem[f"xl{c}"], 16)
                    for t in range(24):
                        sum_square(n, t)
                        norm_at(n, t - 15)
                        if t % 12 >= 8:
                            lo_unit(sec, None, 4 * (t // 12) + t % 4, t % 4)
                else:
                    with runs(pool, sec) as i:
                        for t in range(12):
                            if t >= 8:
                                lo_unit(sec, i, t - 8, t - 8)
                            if sec.f == 0:
                                norm_at(1 + 2 * sec.layer, NORM_ON + t)
                        for t in range(12):
                            if sec.last:
                                sum_square(2 + 2 * sec.layer, 2 * t)
                                sum_square(2 + 2 * sec.layer, 2 * t + 1)
                                norm_at(2 + 2 * sec.layer, t - 3)
                            if t >= 8 and t - 8 < sec.nxt:
                                lo_unit(sec, i, 4 + t - 8, t - 8)
                    if sec.last and sec.layer == 1:
                        for tick in range(NORM_ON, LAST_TICK + 1):
                            norm_at(4, tick)

        @block.scalar
        def _(act):
            def hi_unit(sec, i, k, u, uses, release):
                st = STAGE[u]
                act.wait_ge(sem[f"ld{st}"], sec.at(i, f"ld{st}", 16 * uses))
                wait(act, "D", release)
                act.copy(WH[u][:, :], WS[st][:, :]).then_inc(sem["whi"], 1)

            def norm(n, c, what):
                w = CHUNKS[c][1]
                if what == "pre_sq":
                    if n == 0:
                        act.wait_ge(sem[f"xl{c}"], 16)
                    else:
                        act.wait_ge(sem["xuP"], nth_of(n, c, "post") + 1)
                    act.activation(ct(ACC, c, 0, 4), ct(XRES, c, 0, 4), ACT.Square).then_inc(sem["sqx"], 1)
                    if n:
                        act.wait_ge(sem["xuD"], nth_of(n, c, "post") + 1)
                    act.activation(ct(ACC, c, 4, 4), ct(XRES, c, 4, 4), ACT.Square).then_inc(sem["sqx"], 1)
                elif what == "pre_hi":
                    for h in range(2):
                        act.wait_ge(sem["hs"], 2 * nth_of(n, c, "pre") + h + 1)
                        act.copy(ct(XH, c, 4 * h, 4), ct(ACC, c, 4 * h, 4)).then_inc(sem["hh"], 1)

            def norm_at(n, tick):
                for c, what in norm_pieces("act", n, tick):
                    norm(n, c, what)

            def square(n, t, src):
                wait(act, "sum", SQUARES * (n - 1) + t - 1)
                return act.activation(SQ[:, t % 2, 0:CHUNKS[square_of(n, t)[0]][1]], src, ACT.Square)

            def empty_qkv(s, bank):
                c, u = s // 3, s % 3
                t0, w = CHUNKS[c]
                if u == 0:
                    act.activation(QT[:, t0:t0 + w], bank[:, 0:w], ACT.Copy, scale=0.125).then_inc(sem["evA"], 1)
                elif u == 1 and c < 2:
                    act.copy(KT[:, t0:t0 + w], bank[:, 0:w]).then_inc(sem["evA"], 1)
                elif u == 1:
                    act.copy(KT[:, t0:N_PROMPT], bank[:, 0:N_PROMPT - t0])
                    act.copy(KT[:, N_PROMPT + N_CACHE:], bank[:, N_PROMPT - t0:w]).then_inc(sem["evA"], 1)
                else:
                    act.copy(VT[:, t0:t0 + w], bank[:, 0:w]).then_inc(sem["evA"], 1)

            first = Section("START", 0, 1, {})
            act.nop().then_inc(sem["xA"], 1)
            norm(0, 0, "pre_sq")
            norm(0, 1, "pre_sq")
            hi_unit(first, None, 0, 0, 1, 0)
            norm(0, 2, "pre_sq")
            norm(0, 0, "pre_hi")
            for u in (1, 2):
                hi_unit(first, None, u, u, 1, 0)
            hi_unit(first, None, 3, 3, 2, 0)
            act.wait_ge(sem["rbias"], 16)
            act.copy(RB1[:, 383:767], RB0[:, 129:513][:, ::-1]).then_inc(sem["rel"], 1)
            act.copy(RB1[:, 767:768], RB0[:, 128:129]).then_inc(sem["rel"], 1)
            act.copy(RB1[:, 0:383], RB0[:, 512:513].to_broadcast([16, 383])).then_inc(sem["rel"], 1)
            act.wait_ge(sem["const"], 96)
            act.wait_ge(sem["rels"], 16)
            for sec in SECTIONS:
                if sec.kind == "T0":
                    for s in range(9):
                        act.wait_ge(sem["D"], sec.at(None, "D", s + 1))
                        empty_qkv(s, ps[:, s % 6, :])
                        if sec.layer == 0 and s in (0, 2):
                            norm(0, 1 + s // 2, "pre_hi")
                        if s >= 6:
                            hi_unit(sec, None, s - 6, s - 6, 1, sec.at(None, "D", s + 1))
                        if sec.layer == 1:
                            norm_at(2, NORM_ON + s)
                    if sec.layer == 0:
                        for c, (t0, w) in enumerate(CHUNKS):
                            act.wait_ge(sem["D"], 10 + c)
                            act.activation(ZF[:, t0:t0 + w], ps[0:8, (9 + c) % 6, 0:w], ACT.Identity, bias=bF[:, 0:1])\
                                .then_inc(sem["evA"], 1)
                        act.wait_ge(sem["lamdot"], 2)
                        act.activation(LP[:, :], LP[:, :], ACT.Exp).then_inc(sem["lamexp"], 1)
                        act.wait_ge(sem["fabs"], 1)
                        act.activation(FA[:, 0:TOK], FA[:, 0:TOK], ACT.Exp, scale=-1.0).then_inc(sem["fexp"], 1)
                        act.wait_ge(sem["fexp"], 1)
                        act.activation(FA[:, 0:TOK], FA[:, 0:TOK], ACT.Ln, bias=1.0).then_inc(sem["flog"], 1)
                elif sec.kind == "ATT":
                    kind = sec.att
                    pace = kind if sec.proj else "alone"
                    if sec.g0 % GROUPS == 0:
                        norms_over(act, sec)
                        act.wait_ge(sem["lam"], 1)
                    with runs(act, sec) as i:
                        def empty(use):
                            act.wait_ge(sem["xpe"], sec.at(i, "xpe", use.n + 1))
                            bank = ps[:, 6 + use.bank, :]
                            if use.what == "OT":
                                q0 = block_of(kind, use.block)[0]
                                w = N_SAMPLE if use.block == SAMPLE else P
                                if kind == "A":
                                    act.activation(OT[:, q0:q0 + w], bank[:, 0:w], ACT.Copy, scale=subg[:, 0:1]).then_inc(sem["xA"], 1)
                                else:
                                    act.copy(OT[:, q0:q0 + w], bank[:, 0:w]).then_inc(sem["xA"], 1)
                                return
                            for dst, src in transposed(use, bank):
                                ins = act.copy(dst, src)
                            ins.then_inc(sem["xA"], 1)

                        def exps(s, m):
                            n, q = block_of(kind, ORDER[s])[2], 2 * (s % 2) + m
                            act.wait_ge(sem["nm"], sec.at(i, "nm", 2 * s + m + 1))
                            act.activation(PR[:, s % 2, m, 0:n], PR[:, s % 2, m, 0:n], ACT.Exp, bias=NM[:, q:q + 1],
                                           accum_out=L[:, q:q + 1]).then_inc(sem["ex"], 1)

                        def empty_dense(s):
                            u = s % 3
                            act.wait_ge(sem["D"], sec.at(i, "D", s + 1))
                            if u == 0:
                                act.wait_ge(sem["qklo"], sec.at(i, "qklo", 1))
                            elif u == 1:
                                act.wait_ge(sem["qklo"], sec.at(i, "qklo", 2))
                                act.wait_ge(sem["kst"], sec.at(i, "kst", 16))
                            else:
                                act.wait_ge(sem["vst"], sec.at(i, "vst", 16))
                                act.wait_ge(sem["xpe"], sec.at(i, "xpe", 3))
                            empty_qkv(s, ps[:, s % 2, :])

                        def output_hi(o):
                            if o < 7:
                                act.wait_ge(sem[f"os{o % 2}"], sec.at(i, f"os{o % 2}", 16 * (o // 2 + 1)))
                            else:
                                act.wait_ge(sem["xA"], sec.at(i, "xA", sec.per["xA"]))
                            act.wait_ge(sem["D"], sec.at(i, "D"))
                            src = (QT, VT)[o % 2] if o < 7 else OT
                            for c, (t0, w) in enumerate(CHUNKS):
                                ins = act.copy(ct(XH, c, o), src[:, t0:t0 + w])
                            ins.then_inc(sem["ohi"], 1)

                        wait(act, "S", sec.at(i, "S"))
                        act.wait_ge(sem["evA"], sec.at(i, "evA"))
                        act.copy(Qh[:, 0:TOK], QT[:, :]).then_inc(sem["qkhi"], 1)
                        act.wait_ge(sem["kc"], sec.at(i, "kc"))
                        act.copy(Kh[:, :], KT[:, :]).then_inc(sem["qkhi"], 1)
                        if not sec.proj:
                            hi_unit(sec, i, 0, 3, 1, 0)
                        for s in range(11):
                            mine = [use for use in USES[kind][0][s] if use.engine == "A"]
                            ts = [use for use in mine if use.what != "OT"]
                            ots = [use for use in mine if use.what == "OT"]
                            early = 0 < s < 9 and S_AT[pace][s] < 12
                            if early:
                                exps(s, 0)
                                for use in ts[:1]:
                                    empty(use)
                                exps(s, 1)
                                ts = ts[1:]
                            for use in ts:
                                empty(use)
                            if s < 9 and not early:
                                exps(s, 0)
                                exps(s, 1)
                            for use in ots:
                                empty(use)
                            if sec.proj and (s < 8 or s == 10):
                                step = min(s, 8)
                                empty_dense(step)
                                if step >= 6:
                                    hi_unit(sec, i, step - 6, step - 6, 1, sec.at(i, "D", step + 1))
                            if not sec.proj and 1 <= s < 8:
                                output_hi(s - 1)
                        if not sec.proj:
                            output_hi(7)
                elif sec.kind == "OUT":
                    for t in range(24):
                        q, c, u = t // 12, t % 12 // 4, t % 4
                        w = CHUNKS[c][1]
                        act.wait_ge(sem["D"], sec.at(None, "D", t + 1))
                        square(1 + 2 * sec.layer, t, ps[:, t % 6, 0:w]).then_inc(sem["sqo"], 1)
                        act.copy(ct(ACC, c, 4 * q + u), ps[:, t % 6, 0:w]).then_inc(sem["evA"], 1)
                        if c == 2:
                            uses = (2 if STAGE[u] == 0 else 1) * q + (2 if u == 3 else 1)
                            hi_unit(sec, None, 4 * q + u, u, uses, sec.at(None, "D", t + 1))
                        norm_at(1 + 2 * sec.layer, t - 15)
                else:
                    with runs(act, sec) as i:
                        for t in range(12):
                            c, u = t // 4, t % 4
                            w = CHUNKS[c][1]
                            act.wait_ge(sem["D"], sec.at(i, "D", t + 1))
                            if t >= 2 or sec.base.get("um", 0):
                                act.wait_ge(sem["um"], sec.at(i, "um", t - 1))
                            act.activation(TU[:, t % 2, 0:w], ps[:, t % 6, 0:w], ACT.Relu).then_inc(sem["evA"], 1)
                            act.wait_ge(sem["evA"], sec.at(i, "evA", t + 1))
                            if sec.f == 0:
                                act.wait_ge(sem[f"xst{c}"], 16 * (1 + 2 * sec.layer))
                            act.activation(ct(U, c, u), TU[:, t % 2, 0:w], ACT.Square).then_inc(sem["uhi"], 1)
                            if c == 2:
                                hi_unit(sec, i, u, u, 2 if u == 3 else 1, sec.at(i, "D", t + 1))
                            if sec.f == 0:
                                norm_at(1 + 2 * sec.layer, NORM_ON + t)
                        for t in range(12):
                            c, u = t // 4, t % 4
                            for v in (2 * t, 2 * t + 1) if sec.last else ():
                                act.wait_ge(sem["evD"], sec.at(i, "evD", v + 1))
                                square(2 + 2 * sec.layer, v, ct(ACC, c, v % 8)).then_inc(sem["sqo"], 1)
                            if t >= 8 and u < sec.nxt:
                                uses = {0: 3, 3: 4}.get(u, 2)
                                hi_unit(sec, i, 4 + u, u, uses, sec.at(i, "D", 12 + 2 * (t + 1)))
                            if sec.last:
                                norm_at(2 + 2 * sec.layer, t - 3)
                    if sec.last and sec.layer == 1:
                        for tick in range(NORM_ON, LAST_TICK + 1):
                            norm_at(4, tick)

        @block.vector
        def _(dve):
            def norm(n, c, what):
                part, step = what.split("_")
                w = CHUNKS[c][1]
                j = JOBS.index((n, c, "pre" if step == "lo" else part))
                if step == "red":
                    k = nth_of(n, c, "pre")
                    if k:
                        dve.wait_ge(sem["sta"], [m for m, job in enumerate(JOBS) if job[2] == "pre"][k - 1] + 1)
                    dve.wait_ge(sem["sqx"], 2 * k + 2)
                    dve.tensor_reduce(PSX[:, 0:w], ct(ACC, c, 0, 8).rearrange("p (k w) -> p w k", k=8), AX.X, ALU.add)\
                        .then_inc(sem["ps"], 1)
                elif step == "diag":
                    full, h = w // P, w % P
                    dve.wait_ge(sem["sta"], j + 1)
                    wait(dve, "pw", j)
                    ins = dve.tensor_scalar(ST[:, 0:full], ps[:, 6 + j % 2, 0:full], 1.0 / D_MODEL, EPS, ALU.mult, ALU.add)
                    if h:
                        ins = dve.tensor_scalar(ST[0:h, full:full + 1], ps[0:h, 6 + j % 2, full:full + 1], 1.0 / D_MODEL, EPS, ALU.mult, ALU.add)
                    ins.then_inc(sem["st"], 1)
                    dve.wait_ge(sem["pw"], j + 1)
                    wait(dve, "rb", j - 1)
                    for q in range(full + (h > 0)):
                        v = P if q < full else h
                        ins = dve.tensor_scalar(DG[0:v, j % 2, q * P:q * P + v], ident[0:v, 0:v], RS[0:v, q:q + 1], None, ALU.mult)
                    ins.then_inc(sem["dg"], 1)
                elif step in ("x", "h"):
                    src = ACC if step == "x" else XRES
                    dve.wait_ge(sem["rb"], j + 1)
                    if step == "h" and n:
                        dve.wait_ge(sem["xuP"], nth_of(n, c, "post") + 1)
                        dve.wait_ge(sem["xuD"], nth_of(n, c, "post") + 1)
                    if step == "x" and n % 2:
                        dve.wait_ge(sem["evA"], section("OUT", n // 2).at(None, "evA", 12 + 4 * (c + 1)))
                    for k in range(KT_D):
                        ins = dve.scalar_tensor_tensor(out=ct(ACC, c, k), in0=ct(src, c, k), scalar=gain(NORMS[n][part], k),
                                                       in1=ps[:, 6 + j % 2, 0:w], op0=ALU.mult, op1=ALU.mult)
                        if k % 4 == 3:
                            ins.then_inc(sem["hs" if step == "h" else "xs"], 1)
                    if step == "x":
                        dve.wait_ge(sem["xs"], 2 * nth_of(n, c, "post") + 2)
                        dve.wait_ge(sem[f"xl{c}"], 16 * (n + 1))
                        dve.tensor_tensor(ct(XRES, c, 4, 4), ct(XRES, c, 4, 4), ct(ACC, c, 4, 4), ALU.add).then_inc(sem["xuD"], 1)
                elif step == "lo":
                    dve.wait_ge(sem["hh"], 2 * nth_of(n, c, "pre") + 2)
                    dve.tensor_tensor(ct(XL, c, 4, 4), ct(ACC, c, 4, 4), ct(XH, c, 4, 4).bitcast(f32), ALU.subtract)\
                        .then_inc(sem["hlD"], 1)

            def norm_at(n, tick):
                for c, what in norm_pieces("dve", n, tick):
                    norm(n, c, what)

            for name in ("ttr", "xD"):
                dve.nop().then_inc(sem[name], 1)
            dve.wait_ge(sem["const"], 96)
            dve.tensor_scalar(subg[:, :], subg[:, :], 1.0 - LAM_INIT, None, ALU.mult).then_inc(sem["lam"], 1)
            for c, what in ((0, "red"), (0, "diag"), (0, "h"), (1, "red"), (0, "lo"), (2, "red"), (1, "diag"),
                             (1, "h"), (1, "lo"), (2, "diag"), (2, "h"), (2, "lo")):
                norm(0, c, "pre_" + what)
            for sec in SECTIONS:
                if sec.kind == "T0" and sec.layer == 0:
                    dve.wait_ge(sem["fl"], 80)
                    for k in range(2):
                        dve.tensor_tensor_reduce(out=LQ[:, 2 * k, :], in0=LQ[:, 2 * k, :], in1=LQ[:, 2 * k + 1, :],
                                                 scale=1.0, scalar=0.0, op0=ALU.mult, op1=ALU.add,
                                                 accum_out=LP[:, k:k + 1]).then_inc(sem["lamdot"], 1)
                    dve.wait_ge(sem["evA"], 12)
                    dve.scalar_tensor_tensor(out=FA[:, 0:TOK], in0=ZF[:, 0:TOK], scalar=-1.0, in1=ZF[:, 0:TOK],
                                             op0=ALU.mult, op1=ALU.max).then_inc(sem["fabs"], 1)
                    dve.memset(ZZ[:, :], 0.0).then_inc(sem["fabs"], 1)
                    dve.wait_ge(sem["lamexp"], 1)
                    dve.tensor_tensor(nlam[:, :], LP[:, 1:2], LP[:, 0:1], ALU.subtract).then_inc(sem["lam"], 1)
                    dve.wait_ge(sem["lam"], 2)
                    dve.tensor_scalar(nlam[:, :], nlam[:, :], -LAM_INIT, None, ALU.add).then_inc(sem["lam"], 1)
                    dve.wait_ge(sem["flog"], 1)
                    for t0, t1, to in ((0, N_PROMPT, 0), (N_PROMPT, TOK, N_PROMPT + N_CACHE)):
                        dve.scalar_tensor_tensor(out=LF[:, to:to + t1 - t0], in0=ZF[:, t0:t1], scalar=0.0, in1=FA[:, t0:t1],
                                                 op0=ALU.min, op1=ALU.subtract).then_inc(sem["flogf"], 1)
                    dve.wait_ge(sem["flogf"], 2)
                    dve.wait_ge(sem["fabs"], 2)
                    for t0, t1 in ((0, N_PROMPT), (N_PROMPT, KCOLS)):
                        dve.tensor_tensor_scan(NC[:, t0:t1], ZZ[:, t0:t1], LF[:, t0:t1], 0.0, ALU.add, ALU.subtract)\
                            .then_inc(sem["fscan"], 1)
                elif sec.kind == "T0":
                    for tick in range(NORM_ON, LAST_TICK + 1):
                        norm_at(2, tick)
                elif sec.kind == "ATT":
                    kind = sec.att
                    pace = kind if sec.proj else "alone"
                    if sec.g0 % GROUPS == 0:
                        norms_over(dve, sec)
                        if sec.layer == 0:
                            dve.wait_ge(sem["lam"], 3)
                    with runs(dve, sec) as i:
                        def scores(s, m):
                            _, _, n, b0 = block_of(kind, ORDER[s])
                            q = 2 * (s % 2) + m
                            dve.wait_ge(sem["S"], sec.at(i, "S", 2 * s + m + 1))
                            dve.memset(hold[:, :], 0.0)
                            nb = banks_of(n)
                            dve.tensor_tensor_reduce(
                                out=PR[:, s % 2, m, 0:n].rearrange("p (b w) -> p b w", b=nb), in0=ps[:, 2 + 2 * m:2 + 2 * m + nb, 0:n // nb],
                                in1=BIAS[:, 0 if kind == "A" else m, b0:b0 + n].rearrange("p (b w) -> p b w", b=nb), scale=1.0, scalar=-3.0e38,
                                op0=ALU.add, op1=ALU.max, accum_out=M[:, q:q + 1]).then_inc(sem["ttr"], 1)
                            dve.wait_ge(sem["ttr"], sec.at(i, "ttr", 2 * s + m + 1))
                            dve.tensor_scalar(NM[:, q:q + 1], M[:, q:q + 1], -1.0, None, ALU.mult).then_inc(sem["nm"], 1)

                        def set_free(s):
                            if s < 2:
                                wait(dve, "xpe", sec.at(i, "xpe"))
                            else:
                                last = [use for use in USES[kind][1] if use.what == "T" and use.block == ORDER[s - 2]][-1]
                                dve.wait_ge(sem["xpe"], sec.at(i, "xpe", last.n + 1))

                        def empty(use, s):
                            dve.wait_ge(sem["xpe"], sec.at(i, "xpe", use.n + 1))
                            bank = ps[:, 6 + use.bank, :]
                            if use.what != "PV":
                                for dst, src in transposed(use, bank):
                                    ins = dve.tensor_copy(dst, src)
                                ins.then_inc(sem["xD"], 1)
                                return
                            k, q = s - 1, 2 * ((s - 1) % 2)
                            dve.wait_ge(sem["ri"], sec.at(i, "ri", k + 1))
                            if kind != "A":
                                dve.tensor_scalar(ON[:, 0:64], bank[:, 0:64], RI[:, q:q + 1], None, ALU.mult)
                                dve.tensor_scalar(ON[:, 64:P], bank[:, 64:P], RI[:, q + 1:q + 2], None, ALU.mult).then_inc(sem["xD"], 1)
                                return
                            dve.tensor_scalar(ON[:, :], bank[:, 0:P], RI[:, q:q + 1], None, ALU.mult).then_inc(sem["xD"], 1)
                            dve.wait_ge(sem["xD"], sec.at(i, "xD", use.nth))
                            dve.tensor_tensor_reduce(out=SQ[:, 0, 0:P], in0=ON[:, :], in1=ON[:, :], scale=1.0 / P, scalar=EPS,
                                                     op0=ALU.mult, op1=ALU.add, accum_out=MS[:, k % 2:k % 2 + 1]).then_inc(sem["ms"], 1)

                        def sums(s):
                            q, n = 2 * (s % 2), block_of(kind, ORDER[s])[2]
                            dve.wait_ge(sem["ex"], sec.at(i, "ex", 2 * s + 2))
                            dve.reciprocal(RI[:, q:q + 2], L[:, q:q + 2]).then_inc(sem["ri"], 1)
                            if kind == "A":
                                dve.wait_ge(sem["ri"], sec.at(i, "ri", s + 1))
                                dve.scalar_tensor_tensor(out=CS[:, s % 2:s % 2 + 1], in0=L[:, q:q + 1], scalar=RI[:, q + 1:q + 2],
                                                         in1=nlam[:, 0:1], op0=ALU.mult, op1=ALU.mult).then_inc(sem["cs"], 1)
                                dve.wait_ge(sem["cs"], sec.at(i, "cs", s + 1))
                                dve.scalar_tensor_tensor(out=PR[:, s % 2, 0, 0:n], in0=PR[:, s % 2, 1, 0:n], scalar=CS[:, s % 2:s % 2 + 1],
                                                         in1=PR[:, s % 2, 0, 0:n], op0=ALU.mult, op1=ALU.add).then_inc(sem["comb"], 1)

                        def normed(k):
                            dve.wait_ge(sem["rs"], sec.at(i, "rs", k + 1))
                            dve.tensor_scalar(ON[:, :], ON[:, :], RSO[:, k % 2:k % 2 + 1], None, ALU.mult).then_inc(sem["on2"], 1)

                        dve.wait_ge(sem["qkhi"], sec.at(i, "qkhi", 1))
                        dve.tensor_tensor(Ql[:, 0:TOK], QT[:, :], Qh[:, 0:TOK].bitcast(f32), ALU.subtract).then_inc(sem["qklo"], 1)
                        dve.wait_ge(sem["qkhi"], sec.at(i, "qkhi", 2))
                        dve.tensor_tensor(Kl[:, :], KT[:, :], Kh[:, :].bitcast(f32), ALU.subtract).then_inc(sem["qklo"], 1)
                        dve.wait_ge(sem["bias"], sec.at(i, "bias", sec.per["bias"]))
                        if kind == "C":
                            for m in range(2):
                                dve.memset(BIAS[0:64, m, C_BAND - 64:C_BAND], NEG)
                                ins = dve.memset(BIAS[64:P, m, 0:64], NEG)
                            ins.then_inc(sem["cm"], 1)
                            dve.wait_ge(sem["cm"], sec.at(i, "cm", 1))
                        for s in range(11):
                            mine = [use for use in USES[kind][0][s] if use.engine == "D"]
                            early = 0 < s < 9 and S_AT[pace][s] < 12
                            if early:
                                set_free(s)
                                scores(s, 0)
                                scores(s, 1)
                            for use in mine:
                                if use.what != "PV":
                                    empty(use, s)
                            if s < 9 and not early:
                                set_free(s)
                                scores(s, 0)
                                scores(s, 1)
                            for use in mine:
                                if use.what == "PV":
                                    empty(use, s)
                            if s < 9:
                                sums(s)
                            if kind == "A" and 1 <= s <= 9:
                                normed(s - 1)
                elif sec.kind == "OUT":
                    for t in range(24):
                        norm_at(1 + 2 * sec.layer, t - 15)
                elif sec.kind == "FF":
                    with runs(dve, sec) as i:
                        for t in range(12):
                            c, u = t // 4, t % 4
                            w = CHUNKS[c][1]
                            dve.wait_ge(sem["evA"], sec.at(i, "evA", t + 1))
                            dve.tensor_tensor(TS[:, t % 2, 0:w], TU[:, t % 2, 0:w], TU[:, t % 2, 0:w], ALU.mult).then_inc(sem["um"], 1)
                            dve.wait_ge(sem["um"], sec.at(i, "um", t + 1))
                            dve.wait_ge(sem["uhi"], sec.at(i, "uhi", t + 1))
                            dve.tensor_tensor(ct(U, c, 4 + u), TS[:, t % 2, 0:w], ct(U, c, u).bitcast(f32), ALU.subtract)\
                                .then_inc(sem["uu"], 1)
                            if sec.f == 0:
                                norm_at(1 + 2 * sec.layer, NORM_ON + t)
                        for t in range(12):
                            c, u = t // 4, t % 4
                            w = CHUNKS[c][1]
                            for v in (2 * t, 2 * t + 1):
                                dve.wait_ge(sem["D"], sec.at(i, "D", 12 + v + 1))
                                acc = ct(ACC, c, 2 * u + v % 2)
                                if sec.f == 0:
                                    for name in ("hlP", "hlD"):
                                        dve.wait_ge(sem[name], nth_of(1 + 2 * sec.layer, c, "pre") + 1)
                                    dve.tensor_copy(acc, ps[:, v % 6, 0:w]).then_inc(sem["evD"], 1)
                                else:
                                    dve.wait_ge(sem["evD"], sec.at(i, "evD", v + 1 - 24))
                                    dve.tensor_tensor(acc, ps[:, v % 6, 0:w], acc, ALU.add).then_inc(sem["evD"], 1)
                            if sec.last:
                                norm_at(2 + 2 * sec.layer, t - 3)
                    if sec.last and sec.layer == 1:
                        for tick in range(NORM_ON, LAST_TICK + 1):
                            norm_at(4, tick)

        @block.tensor
        def _(pe):
            def norm(n, c, what):
                part, step = what.split("_")
                w, j = CHUNKS[c][1], JOBS.index((n, c, part))
                if step == "stat":
                    if part == "post":
                        src = PSO[:, CHUNKS[c][0]:CHUNKS[c][0] + w]
                        pe.wait_ge(sem["sum"], SQUARES * (n - 1) + (12 + 4 * (c + 1) if n % 2 else 8 * (c + 1)))
                    else:
                        src = PSX[:, 0:w]
                        pe.wait_ge(sem["ps"], nth_of(n, c, "pre") + 1)
                    if j >= 2:
                        pn, pc, pp = JOBS[j - 2]
                        pe.wait_ge(sem["xs" if pp == "post" else "hs"], 2 * nth_of(pn, pc, pp) + 2)
                    for q in range(-(-w // P)):
                        v = min(P, w - q * P)
                        ins = pe.matmul(ps[0:v, 6 + j % 2, q:q + 1], src[:, q * P:q * P + v], ones[:, 0:1], start=True, stop=True)
                    ins.then_inc(sem["sta"], 1)
                else:
                    pe.wait_ge(sem["dg"], j + 1)
                    for q in range(-(-w // P)):
                        v = min(P, w - q * P)
                        ins = pe.matmul(ps[:, 6 + j % 2, q * P:q * P + v], ones[0:v, :], DG[0:v, j % 2, q * P:q * P + v], start=True, stop=True)
                    ins.then_inc(sem["rb"], 1)

            def norm_at(n, tick):
                for c, what in norm_pieces("pe", n, tick):
                    norm(n, c, what)

            def product(bank, w, c, slot, k, m, src, tiles, lo):
                t, p = m // 3, m % 3
                wt = (WH, WH, WL)[p][slot][:, (k + t) * P:(k + t + 1) * P]
                xt = ct((src, lo[0], src)[p], c, t + (0, lo[1], 0)[p])
                return pe.matmul(bank[:, 0:w], wt, xt, start=m == 0, stop=m == 3 * tiles - 1, skip_group_check=False)

            def step(bank, c, slot, n=None, tick=None):
                for m in range(N_MM):
                    if n is not None and m == N_MM // 2:
                        norm_at(n, tick - 0.5)
                    ins = product(bank, CHUNKS[c][1], c, slot, 0, m, XH, KT_D, (XL, 0))
                ins.then_inc(sem["D"], 1)
                if n is not None:
                    norm_at(n, tick)

            def weights(sec, i, u):
                per = {"ATT": 3, "FF": 8}.get(sec.kind, 0)
                pe.wait_ge(sem["wlo"], sec.pick(i, sec.unit + u + 1, per))

            def h_ready(n, c):
                pe.wait_ge(sem["hlD"], nth_of(n, c, "pre") + 1)
                pe.wait_ge(sem["hlP"], nth_of(n, c, "pre") + 1)

            for name in ("S", "xpe"):
                pe.nop().then_inc(sem[name], 1)
            pe.wait_ge(sem["ones"], 2)
            norm(0, 0, "pre_stat")
            norm(0, 0, "pre_bc")
            norm(0, 1, "pre_stat")
            for sec in SECTIONS:
                if sec.kind == "T0":
                    for s in range(3 * sec.units):
                        c, u = (s // 3, s % 3) if s < 9 else (s - 9, 3)
                        if s >= 6:
                            pe.wait_ge(sem["evA"], sec.at(None, "evA", s - 5))
                        else:
                            wait(pe, "evD", sec.at(None, "evD", s - 5))
                        if c == 0:
                            weights(sec, None, u)
                        if u == 0:
                            h_ready(2 * sec.layer, c)
                        if sec.layer == 1:
                            step(ps[:, s % 6, :], c, u, 2, NORM_ON + s)
                        else:
                            step(ps[:, s % 6, :], c, u)
                        if sec.layer == 0 and s < 3:
                            norm(0, *((1, "pre_bc"), (2, "pre_stat"), (2, "pre_bc"))[s])
                elif sec.kind == "ATT":
                    kind = sec.att
                    pace = kind if sec.proj else "alone"
                    if sec.g0 % GROUPS == 0:
                        pe.wait_ge(sem["pad"], 2 * (sec.layer + 1))
                        pe.wait_ge(sem["hs"], 2 * nth_of(2 * sec.layer, 2, "pre") + 2)
                    with runs(pe, sec) as i:
                        def scores(s, m):
                            q0, k0, n, _ = block_of(kind, ORDER[s])
                            wait(pe, "ttr", sec.at(i, "ttr", 2 * (s - 1) + m + 1 if s else 0))
                            if s == 0:
                                pe.wait_ge(sem["qklo"], sec.at(i, "qklo", 2))
                            rows = slice(64 * m, 64 * m + 64)
                            w = n // banks_of(n)
                            for b, o in enumerate(range(0, n, w)):
                                out = ps[:, 2 + 2 * m + b, :]
                                q, k = slice(q0, q0 + P), slice(k0 + o, k0 + o + w)
                                pe.matmul(out[:, 0:w], Qh[rows, q], Kh[rows, k], start=True, stop=False)
                                if kind == "B" and o + w == n:
                                    v = N_SAMPLE if ORDER[s] == SAMPLE else P
                                    pe.matmul(out[:, w - v:w], identb[:, :], trib[:, 0:v], start=False, stop=False)
                                pe.matmul(out[:, 0:w], Qh[rows, q], Kl[rows, k], start=False, stop=False)
                                ins = pe.matmul(out[:, 0:w], Ql[rows, q], Kh[rows, k], start=False, stop=True)
                            ins.then_inc(sem["S"], 1)

                        def use_bank(use, s):
                            if use.prev is None:
                                wait(pe, "xA", sec.at(i, "xA"))
                                wait(pe, "xD", sec.at(i, "xD"))
                            else:
                                name = "x" + use.prev.engine
                                pe.wait_ge(sem[name], sec.at(i, name, use.prev.nth))
                            bank = ps[:, 6 + use.bank, :]
                            if use.what == "V":
                                pe.wait_ge(sem["evA"], sec.at(i, "evA"))
                                for k, t in enumerate(use.tiles):
                                    t0, v = (t * P, P) if t < 8 else (N_PROMPT, N_SAMPLE)
                                    ins = pe.transpose(bank[0:v, k * P:(k + 1) * P], VT[:, t0:t0 + v], ident[:, :])
                            elif use.what == "T":
                                k, st = s - 1, (s - 1) % 2
                                if kind == "A":
                                    pe.wait_ge(sem["comb"], sec.at(i, "comb", k + 1))
                                else:
                                    pe.wait_ge(sem["ex"], sec.at(i, "ex", 2 * k + use.m + 1))
                                for n, (o, v, _) in enumerate(use.tiles):
                                    ins = pe.transpose(bank[0:v, n * P:(n + 1) * P], PR[:, st, use.m, o:o + v], ident[:, :])
                            elif use.what == "OT":
                                k = s - 2
                                if kind == "A":
                                    pe.wait_ge(sem["on2"], sec.at(i, "on2", k + 1))
                                else:
                                    pv = [v for v in USES[kind][1] if v.what == "PV" and v.block == use.block][0]
                                    pe.wait_ge(sem["xD"], sec.at(i, "xD", pv.nth))
                                ins = pe.transpose(bank[:, 0:P], ON[:, :], ident[:, :])
                            else:
                                before = [v for v in USES[kind][1][:use.n] if v.what in ("V", "T")]
                                for e in "AD":
                                    nth = max(v.nth for v in before if v.engine == e)
                                    pe.wait_ge(sem["x" + e], sec.at(i, "x" + e, nth))
                                if use.block == SAMPLE:
                                    pe.wait_ge(sem["vc"], sec.at(i, "vc", 16))
                                for m in range(1 if kind == "A" else 2):
                                    f = slice(0, P) if kind == "A" else slice(64 * m, 64 * m + 64)
                                    for n, (o, v, t) in enumerate(use.tiles):
                                        ins = pe.matmul(bank[:, f], PT[0:v, m, o // P, :], V[0:v, t, f],
                                                        start=n == 0, stop=n == len(use.tiles) - 1)
                            ins.then_inc(sem["xpe"], 1)

                        for s in range(11):
                            m0, m1 = SLOT_PRODUCTS[s] if sec.proj else (0, N_MM)
                            uses = USES[kind][0][s]
                            early = [use for use in uses if use.what in ("T", "V")]
                            t0, t1 = T_AT[pace][s]
                            at = {use: t0 + (t1 - t0) * k // len(early) for k, use in enumerate(early)}
                            at.update({use: m1 for use in uses if use not in early})
                            if s < 9 and sec.proj:
                                c, u = s // 3, s % 3
                                if s == 0:
                                    pe.wait_ge(sem["evA"], sec.at(i, "evA"))
                                elif s >= 2:
                                    pe.wait_ge(sem["evA"], sec.at(i, "evA", s - 1))
                                if c == 0:
                                    weights(sec, i, u)
                            for m in range(m0, m1 + 1):
                                if s < 9 and S_AT[pace][s] == m:
                                    scores(s, 0)
                                    scores(s, 1)
                                for use in uses:
                                    if at[use] == m:
                                        use_bank(use, s)
                                if sec.proj and m < m1:
                                    ins = product(ps[:, min(s, 8) % 2, :], CHUNKS[c][1], c, u, 0, m, XH, KT_D, (XL, 0))
                                    if m == N_MM - 1:
                                        ins.then_inc(sem["D"], 1)
                elif sec.kind == "OUT":
                    pe.wait_ge(sem["evA"], sec.at(None, "evA"))
                    for name in ("ttr", "xA", "xD", "olo"):
                        pe.wait_ge(sem[name], sec.at(None, name))
                    for t in range(24):
                        q, c, u = t // 12, t % 12 // 4, t % 4
                        if t >= 6:
                            pe.wait_ge(sem["evA"], sec.at(None, "evA", t - 5))
                        if c == 0:
                            weights(sec, None, 4 * q + u)
                        step(ps[:, t % 6, :], c, u, 1 + 2 * sec.layer, t - 15)
                else:
                    with runs(pe, sec) as i:
                        for t in range(12):
                            c, u = t // 4, t % 4
                            if t >= 6 or sec.f == 0:
                                pe.wait_ge(sem["evA"], sec.at(i, "evA", t - 5))
                            else:
                                pe.wait_ge(sem["evD"], sec.at(i, "evD", t - 5))
                            if c == 0:
                                weights(sec, i, u)
                            if sec.f == 0 and u == 0:
                                h_ready(1 + 2 * sec.layer, c)
                            if sec.f == 0:
                                step(ps[:, t % 6, :], c, u, 1 + 2 * sec.layer, NORM_ON + t)
                            else:
                                step(ps[:, t % 6, :], c, u)
                        for t in range(12):
                            c, u = t // 4, t % 4
                            if c == 0:
                                weights(sec, i, 4 + u)
                            if u == 0:
                                pe.wait_ge(sem["uu"], sec.at(i, "uu", 4 * (c + 1)))
                            for v in (2 * t, 2 * t + 1):
                                if v < 6:
                                    pe.wait_ge(sem["evA"], sec.at(i, "evA", 7 + v))
                                else:
                                    pe.wait_ge(sem["evD"], sec.at(i, "evD", v - 5))
                                for m in range(N_MM // 2):
                                    ins = product(ps[:, v % 6, :], CHUNKS[c][1], c, u, 4 * (v % 2), m, U, 4, (U, 4))
                                ins.then_inc(sem["D"], 1)
                                if sec.last:
                                    norm_at(2 + 2 * sec.layer, t - 3 if v % 2 else t - 3.5)
                    if sec.last and sec.layer == 1:
                        for tick in range(NORM_ON, LAST_TICK + 1):
                            norm_at(4, tick - 0.5)
                            norm_at(4, tick)


def kernel(**inputs):
    import numpy as np
    import ml_dtypes
    import concourse.bacc as bacc
    from concourse.bass_utils import run_bass_kernel_spmd as run

    a = {name: np.asarray(v) for name, v in inputs.items()}

    def feature_major(x):
        t = x.T.reshape(KT_D, P, TOK).transpose(1, 0, 2)
        return np.concatenate([t[:, :, o:o + w].reshape(P, -1) for o, w in CHUNKS], axis=1)

    def unit(w):
        return w.reshape(KT_D, P, P).transpose(1, 0, 2).reshape(1, P, KT_D * P)

    def columns(w, c0):
        return unit(w[:, c0:c0 + P])

    def mlp_units(up, down):
        out = []
        for f in range(FF_GROUPS):
            out += [columns(up, (4 * f + u) * P) for u in range(4)]
            d = down[4 * P * f:4 * P * (f + 1)].reshape(4, P, 4, 2, P)
            out += [d[:, :, u].transpose(1, 2, 0, 3).reshape(1, P, -1) for u in range(4)]
        return out

    we, wo = a["w_in_even"][0], a["w_in_odd"][0]
    qk, v0 = 512, 1024
    cols = [(h * P, qk + h * P, v0 + h * P) for h in range(4)] + [(1536 + j * P, 2048 + j * P, 2560 + j * P) for j in range(4)]
    units = [columns(we, c) for c in cols[0]]
    gate = np.zeros((D_MODEL, P), np.float32)
    gate[:, 0:8] = we[:, 3072:3080]
    units.append(unit(gate))
    units += [columns(we, c) for group in cols[1:] for c in group]
    units += [columns(a["w_out_even"][0], o * P) for o in range(8)] + mlp_units(a["w_ffn_up"][0], a["w_ffn_down"][0])
    units += [columns(wo, s * D_MODEL + j * P) for j in range(8) for s in range(3)]
    units += [columns(a["w_out_odd"][0], o * P) for o in range(8)] + mlp_units(a["w_ffn_up"][1], a["w_ffn_down"][1])
    assert len(units) == UNITS

    gains = np.concatenate([a["g_" + which][layer].reshape(KT_D, P).T for which, layer in GAINS], axis=1)

    def k_tiles(cache, n):
        return cache.reshape(N_CACHE, n, P).transpose(1, 2, 0)

    def v_tiles(cache, n):
        return cache.reshape(2, P, n, P).transpose(2, 1, 0, 3)

    kcache = np.concatenate([k_tiles(a["cache_a_k"][0, 0], 4), k_tiles(a["cache_b_k"][0, 0], 4), k_tiles(a["cache_c_k"][0, 0], 8)])
    vcache = np.concatenate([v_tiles(a["cache_a_v"][0, 0], 4), v_tiles(a["cache_b_v"][0, 0], 4), v_tiles(a["cache_c_v"][0, 0], 8)])
    q, k = np.arange(P)[:, None], np.arange(1024)[None, :] - (1024 - P)
    dist = np.where(k // 64 <= q // 64, -np.abs(q - k).astype(np.float32), 0)
    alibi = np.stack([np.where(k // 64 <= q // 64, dist * 2.0 ** (-8.0 * (h + 1) / 4), NEG) for h in range(4)]).astype(np.float32)
    causal = np.where(np.arange(P)[None, :] <= np.arange(P)[:, None], 0, NEG).astype(ml_dtypes.bfloat16)
    x = np.concatenate([a["x_prompt"][0], a["x_sample"][0]])
    arrays = dict(
        x_in=feature_major(x), w_in=np.concatenate(units), gains_in=gains, subg_in=a["subln_g"][0].reshape(P, 1),
        bf_in=a["b_forget"][0].reshape(8, 1), lam_in=np.concatenate([a[n] for n in ("lam_q1", "lam_k1", "lam_q2", "lam_k2")]),
        kcache=kcache, vcache=vcache, logf_cache=a["cache_b_logf"][0, 0].T, alibi=alibi, rel_bias=a["rel_bias"][0],
        ident_in=np.eye(P, dtype=np.float32), identb_in=np.eye(P).astype(ml_dtypes.bfloat16), tri_in=causal)
    outputs = dict(y_out=(P, 8 * TOK), k_out=(16, P, KCOLS), v_out=(16, P, TOK), logf_out=(8, TOK), vband_out=(8, P, 2, P))

    nc = bacc.Bacc("TRN2", target_bir_lowering=False, num_devices=1)
    args = {}
    for name, v in arrays.items():
        arrays[name] = v = np.ascontiguousarray(v)
        args[name] = nc.dram_tensor(name, v.shape, mybir.dt.from_np(v.dtype), kind="ExternalInput").ap()
    for name, shape in outputs.items():
        args[name] = nc.dram_tensor(name, shape, mybir.dt.float32, kind="ExternalOutput").ap()
    build_program(nc, **args)
    r = run(nc, [arrays], core_ids=[0]).results[0]

    y = r["y_out"]
    y = np.concatenate([y[:, 8 * o:8 * (o + w)].reshape(P, KT_D, w) for o, w in CHUNKS], axis=2)
    y = y.transpose(2, 1, 0).reshape(TOK, D_MODEL)

    def rows(t, heads):
        n = t.shape[2]
        return t.transpose(2, 0, 1).reshape(1, 1, n, heads, -1)

    kk, vv = r["k_out"], r["v_out"]
    kp, ks, vp, vs = kk[:, :, 0:N_PROMPT], kk[:, :, N_PROMPT + N_CACHE:], vv[:, :, 0:N_PROMPT], vv[:, :, N_PROMPT:]
    lf = r["logf_out"]
    v_past = r["vband_out"].transpose(0, 3, 2, 1).reshape(8, P, N_CACHE)
    band_v = np.concatenate([v_past[:, :, N_SAMPLE:], vs[8:]], axis=2)
    return (y[None, 0:N_PROMPT], y[None, N_PROMPT:],
            rows(kp[0:4], 4), rows(vp[0:4], 4), rows(kp[4:8], 8), rows(vp[4:8], 8), lf[:, 0:N_PROMPT].T[None, None],
            rows(kp[8:, :, 512:], 16), rows(vp[8:, :, 512:], 16),
            rows(ks[0:4], 4), rows(vs[0:4], 4), rows(ks[4:8], 8), rows(vs[4:8], 8), lf[:, N_PROMPT:].T[None, None],
            rows(kk[8:, :, N_PROMPT + N_SAMPLE:], 16), rows(band_v, 16))
```
